# Optimizing a Trainium2 kernel written in Bass

```python
import math
import jax
import jax.numpy as jnp
from jax import lax
import numpy as np
import jax, jax.numpy as jnp

D_MODEL = 1024
BATCH = 1
SEQ = 256
DEPTH = 1

N_HEADS = 8
HEAD_DIM = 64
ATTN_WIDTH = N_HEADS * HEAD_DIM
MOBA_BLOCK = 256
MOBA_TOPK = 3
MOBA_Q_CHUNK = 64
POOL_WINDOWS = (2, 4, 8, 16)
POOL_GROUPS = len(POOL_WINDOWS)
POOL_WIDTH = D_MODEL // 2
POOL_GROUP_WIDTH = POOL_WIDTH // POOL_GROUPS
N_BRANCHES = 2
IN_WIDTH = 3 * ATTN_WIDTH + POOL_WIDTH + N_BRANCHES * D_MODEL
REL_BUCKETS = 32
REL_MAX_DIST = 128
N_EXPERT_GROUPS = 4
EXPERTS_PER_GROUP = 8
N_EXPERTS = N_EXPERT_GROUPS * EXPERTS_PER_GROUP
EXPERT_TOPK = 2
D_EXPERT = D_MODEL // 2
N_MOD = 6
EPS = 1e-6
NEG_INF = -1e30


def rms_norm(x, g):
    xf = x.astype(jnp.float32)
    xf = xf * lax.rsqrt(jnp.mean(xf * xf, axis=-1, keepdims=True) + EPS)
    return (xf * g.astype(jnp.float32)).astype(x.dtype)

def t5_bucket(rel):
    n = jnp.maximum(rel, 0)
    max_exact = REL_BUCKETS // 2
    nf = jnp.maximum(n, 1).astype(jnp.float32)
    large = max_exact + (jnp.log(nf / max_exact) / math.log(REL_MAX_DIST / max_exact)
                         * (REL_BUCKETS - max_exact)).astype(jnp.int32)
    large = jnp.minimum(large, REL_BUCKETS - 1)
    return jnp.where(n < max_exact, n, large)

def moba_attention(q, k, v, rel_bias):
    B, S, H, Dh = q.shape
    nb = -(-S // MOBA_BLOCK)
    pad = nb * MOBA_BLOCK - S
    topk = min(MOBA_TOPK, nb)
    scale = Dh ** -0.5
    qh = q.transpose(0, 2, 1, 3)
    kp = jnp.pad(k.transpose(0, 2, 1, 3), ((0, 0), (0, 0), (0, pad), (0, 0)))
    vp = jnp.pad(v.transpose(0, 2, 1, 3), ((0, 0), (0, 0), (0, pad), (0, 0)))
    kb = kp.reshape(B, H, nb, MOBA_BLOCK, Dh)
    vb = vp.reshape(B, H, nb, MOBA_BLOCK, Dh)
    k_mean = jnp.mean(kb.astype(jnp.float32), axis=3)
    bias_t = rel_bias.T
    b_idx = jnp.arange(B)[:, None, None, None]
    h_idx = jnp.arange(H)[None, :, None, None]
    h_idx5 = jnp.arange(H)[None, :, None, None, None]
    blk_offsets = jnp.arange(MOBA_BLOCK)

    def attend_chunk(ci):
        q0 = ci * MOBA_Q_CHUNK
        blk = q0 // MOBA_BLOCK
        qc = lax.dynamic_slice_in_dim(qh, q0, MOBA_Q_CHUNK, axis=2)
        qpos = q0 + jnp.arange(MOBA_Q_CHUNK)
        gate = jnp.einsum('bhqd,bhnd->bhqn', qc.astype(jnp.float32), k_mean)
        gate = jnp.where(jnp.arange(nb) < blk, gate, -jnp.inf)
        _, sel = lax.top_k(gate, topk)
        sel_valid = sel < blk
        ks = kb[b_idx, h_idx, sel]
        vs = vb[b_idx, h_idx, sel]
        s_sel = jnp.einsum('bhqd,bhqjkd->bhqjk', qc, ks).astype(jnp.float32) * scale
        kpos_sel = sel[..., None] * MOBA_BLOCK + blk_offsets
        bucket_sel = t5_bucket(qpos[None, None, :, None, None] - kpos_sel)
        s_sel = s_sel + bias_t[h_idx5, bucket_sel].astype(jnp.float32)
        s_sel = jnp.where(sel_valid[..., None], s_sel, NEG_INF)
        ko = lax.dynamic_index_in_dim(kb, blk, axis=2, keepdims=False)
        vo = lax.dynamic_index_in_dim(vb, blk, axis=2, keepdims=False)
        s_own = jnp.einsum('bhqd,bhkd->bhqk', qc, ko).astype(jnp.float32) * scale
        rel_own = qpos[:, None] - (blk * MOBA_BLOCK + blk_offsets)[None, :]
        s_own = s_own + bias_t[:, t5_bucket(rel_own)][None].astype(jnp.float32)
        s_own = jnp.where(rel_own >= 0, s_own, NEG_INF)
        logits = jnp.concatenate(
            [s_sel.reshape(B, H, MOBA_Q_CHUNK, topk * MOBA_BLOCK), s_own], axis=-1)
        p = jax.nn.softmax(logits, axis=-1).astype(v.dtype)
        p_sel = p[..., :topk * MOBA_BLOCK].reshape(B, H, MOBA_Q_CHUNK, topk, MOBA_BLOCK)
        p_own = p[..., topk * MOBA_BLOCK:]
        return (jnp.einsum('bhqjk,bhqjkd->bhqd', p_sel, vs)
                + jnp.einsum('bhqk,bhkd->bhqd', p_own, vo))

    out = lax.map(attend_chunk, jnp.arange(S // MOBA_Q_CHUNK))
    return out.transpose(1, 0, 3, 2, 4).reshape(B, S, H * Dh)

def pool_mixer(u, pool_w, pool_scale):
    B, S, P = u.shape
    uf = u.astype(jnp.float32)
    cs = jnp.pad(jnp.cumsum(uf, axis=1), ((0, 0), (1, 0), (0, 0)))
    t = jnp.arange(S)
    outs = []
    for g, w in enumerate(POOL_WINDOWS):
        lo_c, hi_c = g * POOL_GROUP_WIDTH, (g + 1) * POOL_GROUP_WIDTH
        csg = cs[..., lo_c:hi_c]
        lo = jnp.maximum(t + 1 - w, 0)
        cnt = (t + 1 - lo).astype(jnp.float32)
        mean = (csg[:, 1:] - csg[:, lo]) / cnt[None, :, None]
        d = (mean - uf[..., lo_c:hi_c]).astype(u.dtype)
        outs.append(jnp.einsum('bsc,cd->bsd', d, pool_w[g]))
    return jnp.concatenate(outs, axis=-1) * pool_scale

def hier_moe(h, w_rg, b_rg, w_re, b_re, w_g, w_u, w_d):
    B, S, D = h.shape
    N = B * S
    hf = h.reshape(N, D)
    z_group = (hf @ w_rg).astype(jnp.float32) + b_rg.astype(jnp.float32)
    p_group = jax.nn.softmax(z_group, axis=-1)
    pg_top, g_idx = lax.top_k(p_group, 1)
    z_exp = ((hf @ w_re).astype(jnp.float32) + b_re.astype(jnp.float32)).reshape(
        N, N_EXPERT_GROUPS, EXPERTS_PER_GROUP)
    z_in_group = z_exp[jnp.arange(N), g_idx[:, 0]]
    ze_top, e_idx = lax.top_k(z_in_group, EXPERT_TOPK)
    weights = pg_top * jax.nn.softmax(ze_top, axis=-1)
    expert_id = g_idx * EXPERTS_PER_GROUP + e_idx
    combine = jnp.einsum('nk,nke->ne', weights,
                         jax.nn.one_hot(expert_id, N_EXPERTS, dtype=jnp.float32)).astype(h.dtype)
    y = jnp.zeros_like(hf)
    for e in range(N_EXPERTS):
        act = jax.nn.silu(hf @ w_g[e]) * (hf @ w_u[e])
        y = y + combine[:, e:e + 1] * (act @ w_d[e])
    return y.reshape(B, S, D)

def first_inputs(seed: int = 0) -> dict:
    key = jax.random.key(seed)
    ks = jax.random.split(key, 22)
    f32 = jnp.float32
    D = D_MODEL
    PGW = POOL_GROUP_WIDTH

    def nrm(k, shape, s):
        return jax.random.normal(k, shape, f32) * s

    return {
        "x": nrm(ks[0], (BATCH, SEQ, D), 1.0),
        "c": nrm(ks[1], (BATCH, D), 1.0),
        "w_ada": nrm(ks[2], (DEPTH, D, N_MOD * D), 0.5 * D ** -0.5),
        "b_ada": nrm(ks[3], (DEPTH, N_MOD * D), 0.02),
        "norm1_g": 1.0 + nrm(ks[4], (DEPTH, D), 0.05),
        "w_in": nrm(ks[5], (DEPTH, D, IN_WIDTH), D ** -0.5),
        "b_gate": nrm(ks[6], (DEPTH, N_BRANCHES * D), 0.02),
        "rel_bias": nrm(ks[7], (REL_BUCKETS, N_HEADS), 0.5),
        "pool_w": nrm(ks[8], (DEPTH, POOL_GROUPS, PGW, PGW), PGW ** -0.5),
        "pool_scale": 1.0 + nrm(ks[9], (DEPTH, POOL_WIDTH), 0.1),
        "w_branch_attn": nrm(ks[10], (DEPTH, ATTN_WIDTH, D), ATTN_WIDTH ** -0.5),
        "w_branch_pool": nrm(ks[11], (DEPTH, POOL_WIDTH, D), POOL_WIDTH ** -0.5),
        "w_out": nrm(ks[12], (DEPTH, D, D), D ** -0.5),
        "norm2_g": 1.0 + nrm(ks[13], (DEPTH, D), 0.05),
        "w_router_group": nrm(ks[14], (DEPTH, D, N_EXPERT_GROUPS), D ** -0.5),
        "b_router_group": nrm(ks[15], (DEPTH, N_EXPERT_GROUPS), 0.01),
        "w_router_expert": nrm(ks[16], (DEPTH, D, N_EXPERTS), D ** -0.5),
        "b_router_expert": nrm(ks[17], (DEPTH, N_EXPERTS), 0.01),
        "w_expert_gate": nrm(ks[18], (DEPTH, N_EXPERTS, D, D_EXPERT), D ** -0.5),
        "w_expert_up": nrm(ks[19], (DEPTH, N_EXPERTS, D, D_EXPERT), D ** -0.5),
        "w_expert_down": nrm(ks[20], (DEPTH, N_EXPERTS, D_EXPERT, D), D_EXPERT ** -0.5),
        "norm_f_g": 1.0 + nrm(ks[21], (D,), 0.05),
    }

def first_block(x, c, w_ada, b_ada, norm1_g, w_in, b_gate, rel_bias, pool_w, pool_scale,
              w_branch_attn, w_branch_pool, w_out, norm2_g, w_router_group, b_router_group,
              w_router_expert, b_router_expert, w_expert_gate, w_expert_up, w_expert_down,
              norm_f_g):
    B, S, D = x.shape
    c_act = jax.nn.silu(c)
    split_pts = [ATTN_WIDTH, 2 * ATTN_WIDTH, 3 * ATTN_WIDTH, 3 * ATTN_WIDTH + POOL_WIDTH]
    for l in range(DEPTH):
        mod = (c_act @ w_ada[l] + b_ada[l])[:, None, :]
        shift1, scale1, gate1, shift2, scale2, gate2 = jnp.split(mod, N_MOD, axis=-1)
        h = rms_norm(x, norm1_g[l]) * (1 + scale1) + shift1
        proj = h @ w_in[l]
        q, k, v, u, z_gate = jnp.split(proj, split_pts, axis=-1)
        q = q.reshape(B, S, N_HEADS, HEAD_DIM)
        k = k.reshape(B, S, N_HEADS, HEAD_DIM)
        v = v.reshape(B, S, N_HEADS, HEAD_DIM)
        y_attn = moba_attention(q, k, v, rel_bias) @ w_branch_attn[l]
        y_pool = pool_mixer(u, pool_w[l], pool_scale[l]) @ w_branch_pool[l]
        g_attn, g_pool = jnp.split(jax.nn.sigmoid(z_gate + b_gate[l]), N_BRANCHES, axis=-1)
        mixed = (g_attn * y_attn + g_pool * y_pool) @ w_out[l]
        x = x + gate1 * mixed
        h2 = rms_norm(x, norm2_g[l]) * (1 + scale2) + shift2
        y_moe = hier_moe(h2, w_router_group[l], b_router_group[l], w_router_expert[l],
                         b_router_expert[l], w_expert_gate[l], w_expert_up[l], w_expert_down[l])
        x = x + gate2 * y_moe
    return rms_norm(x, norm_f_g)


V_DIM = 2 * HEAD_DIM
QK_WIDTH = N_HEADS * 2 * HEAD_DIM
ATTN_WIDTH_2 = N_HEADS * V_DIM
Q_BLOCK = 128
SUBLN_EPS = 1e-5
LRU_WIDTH = D_MODEL
LRU_BLOCKS = 16
LRU_BLOCK_W = LRU_WIDTH // LRU_BLOCKS
CONV_WIDTH = 4
LRU_C = 8.0
N_GROUPS = 4
N_EXPERTS_2 = N_GROUPS * EXPERTS_PER_GROUP
TOP_K_INNER = 2
EXPERT_FF = 512
ROUTER_BIAS_SCALE = 0.01
PLE_DIM = 256
NORM_EPS = 1e-6

IN_SIZES = (QK_WIDTH, QK_WIDTH, ATTN_WIDTH_2, LRU_WIDTH, LRU_WIDTH, D_MODEL, D_MODEL)
IN_COLS = sum(IN_SIZES)
IN_SPLITS = tuple(int(s) for s in np.cumsum(IN_SIZES)[:-1])


def rmsnorm(x, g, eps=NORM_EPS):
    xf = x.astype(jnp.float32)
    y = xf * lax.rsqrt(jnp.mean(xf * xf, axis=-1, keepdims=True) + eps)
    return (y * g.astype(jnp.float32)).astype(x.dtype)

def diff_attention(q, k, v, lam):
    B, S = q.shape[0], q.shape[1]
    n_blk = S // Q_BLOCK
    scale = HEAD_DIM ** -0.5
    qb = jnp.moveaxis(q.reshape(B, n_blk, Q_BLOCK, N_HEADS, 2, HEAD_DIM), 1, 0)
    kf = k.astype(jnp.float32)
    vf = v.astype(jnp.float32)
    kpos = jnp.arange(S)
    neg = jnp.finfo(jnp.float32).min

    def one_block(args):
        qi, blk = args
        s = jnp.einsum('bqhcd,bkhcd->bhcqk', qi.astype(jnp.float32), kf) * scale
        qpos = blk * Q_BLOCK + jnp.arange(Q_BLOCK)
        causal = kpos[None, :] <= qpos[:, None]
        s = jnp.where(causal, s, neg)
        pr = jax.nn.softmax(s, axis=-1)
        a = pr[:, :, 0] - lam * pr[:, :, 1]
        return jnp.einsum('bhqk,bkhe->bqhe', a, vf)

    o = lax.map(one_block, (qb, jnp.arange(n_blk)))
    return jnp.moveaxis(o, 0, 1).reshape(B, S, N_HEADS, V_DIM).astype(q.dtype)

def causal_depthwise_conv(x, w, b):
    S = x.shape[1]
    xp = jnp.pad(x, ((0, 0), (CONV_WIDTH - 1, 0), (0, 0)))
    y = b
    for j in range(CONV_WIDTH):
        y = y + xp[:, j:j + S] * w[j]
    return y

def rg_lru(x, w_rg, b_rg, w_ig, b_ig, lru_lambda):
    B, S, W = x.shape
    xb = x.reshape(B, S, LRU_BLOCKS, LRU_BLOCK_W)
    r = jax.nn.sigmoid(jnp.einsum('bsnw,nwv->bsnv', xb, w_rg) + b_rg).reshape(B, S, W)
    ig = jax.nn.sigmoid(jnp.einsum('bsnw,nwv->bsnv', xb, w_ig) + b_ig).reshape(B, S, W)
    log_a = -LRU_C * r.astype(jnp.float32) * jax.nn.softplus(-lru_lambda.astype(jnp.float32))
    a = jnp.exp(log_a)
    mult = jnp.sqrt(-jnp.expm1(2.0 * log_a))
    u = mult * (ig * x).astype(jnp.float32)

    def combine(left, right):
        a_l, b_l = left
        a_r, b_r = right
        return a_l * a_r, a_r * b_l + b_r

    _, h = lax.associative_scan(combine, (a, u), axis=1)
    return h.astype(x.dtype)

def hier_moe_2(h, w_rt_group, b_rt_group, w_rt_expert, b_rt_expert, w_e_gate, w_e_up, w_e_down):
    B, S, D = h.shape
    t = h.reshape(B * S, D)
    grp_logits = (t @ w_rt_group + b_rt_group).astype(jnp.float32)
    grp_prob = jax.nn.softmax(grp_logits, axis=-1)
    g_idx = jnp.argmax(grp_logits, axis=-1)
    g_w = jnp.take_along_axis(grp_prob, g_idx[:, None], axis=1)[:, 0]
    fine = (jnp.einsum('nd,gde->nge', t, w_rt_expert) + b_rt_expert).astype(jnp.float32)
    fine_sel = jnp.take_along_axis(fine, g_idx[:, None, None], axis=1)[:, 0]
    top_logit, top_idx = lax.top_k(fine_sel, TOP_K_INNER)
    top_w = jax.nn.softmax(top_logit, axis=-1)
    expert_id = g_idx[:, None] * EXPERTS_PER_GROUP + top_idx
    weights = g_w[:, None] * top_w
    combine = jnp.sum(jax.nn.one_hot(expert_id, N_EXPERTS_2, dtype=jnp.float32)
                      * weights[..., None], axis=1)

    def expert_step(acc, params):
        wg, wu, wd, c = params
        hid = jax.nn.silu(t @ wg) * (t @ wu)
        return acc + c[:, None] * (hid @ wd).astype(jnp.float32), None

    acc0 = jnp.zeros((B * S, D), jnp.float32)
    y, _ = lax.scan(expert_step, acc0, (w_e_gate, w_e_up, w_e_down, combine.T))
    return y.reshape(B, S, D).astype(h.dtype)

def second_inputs(seed: int = 0) -> dict:
    key = jax.random.key(seed)
    ks = jax.random.split(key, 32)
    f32 = jnp.float32
    L, D = DEPTH, D_MODEL

    def nrm(k, shape, fan_in):
        return jax.random.normal(k, shape, f32) * (fan_in ** -0.5)

    def gain(k, shape):
        return 1.0 + 0.05 * jax.random.normal(k, shape, f32)

    u = jax.random.uniform(ks[16], (L, LRU_WIDTH), f32, 0.9, 0.999)
    s = u ** (1.0 / LRU_C)
    lru_lambda = jnp.log(s) - jnp.log1p(-s)
    return {
        "x": jax.random.normal(ks[0], (BATCH, SEQ, D), f32),
        "p": jax.random.normal(ks[1], (L, BATCH, SEQ, PLE_DIM), f32),
        "g_mix": gain(ks[2], (L, D)),
        "w_in": nrm(ks[3], (L, D, IN_COLS), D),
        "lam_q1": 0.1 * jax.random.normal(ks[4], (L, HEAD_DIM), f32),
        "lam_k1": 0.1 * jax.random.normal(ks[5], (L, HEAD_DIM), f32),
        "lam_q2": 0.1 * jax.random.normal(ks[6], (L, HEAD_DIM), f32),
        "lam_k2": 0.1 * jax.random.normal(ks[7], (L, HEAD_DIM), f32),
        "g_subln": gain(ks[8], (L, V_DIM)),
        "w_conv": nrm(ks[9], (L, CONV_WIDTH, LRU_WIDTH), CONV_WIDTH),
        "b_conv": 0.02 * jax.random.normal(ks[10], (L, LRU_WIDTH), f32),
        "w_rg": nrm(ks[11], (L, LRU_BLOCKS, LRU_BLOCK_W, LRU_BLOCK_W), LRU_BLOCK_W),
        "b_rg": 0.02 * jax.random.normal(ks[12], (L, LRU_BLOCKS, LRU_BLOCK_W), f32),
        "w_ig": nrm(ks[13], (L, LRU_BLOCKS, LRU_BLOCK_W, LRU_BLOCK_W), LRU_BLOCK_W),
        "b_ig": 0.02 * jax.random.normal(ks[14], (L, LRU_BLOCKS, LRU_BLOCK_W), f32),
        "lru_lambda": lru_lambda,
        "w_attn_br": nrm(ks[17], (L, ATTN_WIDTH_2, D), ATTN_WIDTH_2),
        "w_lru_br": nrm(ks[18], (L, LRU_WIDTH, D), LRU_WIDTH),
        "w_out": nrm(ks[19], (L, D, D), D),
        "g_moe": gain(ks[20], (L, D)),
        "w_rt_group": nrm(ks[21], (L, D, N_GROUPS), D),
        "b_rt_group": ROUTER_BIAS_SCALE * jax.random.normal(ks[22], (L, N_GROUPS), f32),
        "w_rt_expert": nrm(ks[23], (L, N_GROUPS, D, EXPERTS_PER_GROUP), D),
        "b_rt_expert": ROUTER_BIAS_SCALE * jax.random.normal(ks[24], (L, N_GROUPS, EXPERTS_PER_GROUP), f32),
        "w_e_gate": nrm(ks[25], (L, N_EXPERTS_2, D, EXPERT_FF), D),
        "w_e_up": nrm(ks[26], (L, N_EXPERTS_2, D, EXPERT_FF), D),
        "w_e_down": nrm(ks[27], (L, N_EXPERTS_2, EXPERT_FF, D), EXPERT_FF),
        "g_ple": gain(ks[28], (L, D)),
        "w_ple_gate": nrm(ks[29], (L, D, D), D),
        "w_ple_proj": nrm(ks[30], (L, PLE_DIM, D), PLE_DIM),
        "g_final": gain(ks[31], (D,)),
    }

def second_block(x, p, g_mix, w_in, lam_q1, lam_k1, lam_q2, lam_k2, g_subln, w_conv, b_conv,
              w_rg, b_rg, w_ig, b_ig, lru_lambda, w_attn_br, w_lru_br, w_out, g_moe,
              w_rt_group, b_rt_group, w_rt_expert, b_rt_expert, w_e_gate, w_e_up, w_e_down,
              g_ple, w_ple_gate, w_ple_proj, g_final):
    B, S = x.shape[0], x.shape[1]
    for i in range(DEPTH):
        lam_init = 0.8 - 0.6 * math.exp(-0.3 * i)
        h = rmsnorm(x, g_mix[i])
        z = h @ w_in[i]
        q, k, v, xr, gr, ga, gb = jnp.split(z, IN_SPLITS, axis=-1)
        q = q.reshape(B, S, N_HEADS, 2, HEAD_DIM)
        k = k.reshape(B, S, N_HEADS, 2, HEAD_DIM)
        v = v.reshape(B, S, N_HEADS, V_DIM)
        lam = (jnp.exp(jnp.sum(lam_q1[i].astype(jnp.float32) * lam_k1[i].astype(jnp.float32)))
               - jnp.exp(jnp.sum(lam_q2[i].astype(jnp.float32) * lam_k2[i].astype(jnp.float32)))
               + lam_init)
        o = diff_attention(q, k, v, lam)
        o = rmsnorm(o, g_subln[i], SUBLN_EPS) * (1.0 - lam_init)
        attn_branch = o.reshape(B, S, ATTN_WIDTH_2) @ w_attn_br[i]
        xc = causal_depthwise_conv(xr, w_conv[i], b_conv[i])
        hr = rg_lru(xc, w_rg[i], b_rg[i], w_ig[i], b_ig[i], lru_lambda[i])
        lru_branch = (hr * jax.nn.gelu(gr)) @ w_lru_br[i]
        mixed = jax.nn.sigmoid(ga) * attn_branch + jax.nn.sigmoid(gb) * lru_branch
        x = x + mixed @ w_out[i]
        x = x + hier_moe_2(rmsnorm(x, g_moe[i]), w_rt_group[i], b_rt_group[i], w_rt_expert[i],
                         b_rt_expert[i], w_e_gate[i], w_e_up[i], w_e_down[i])
        gate = jax.nn.sigmoid(rmsnorm(x, g_ple[i]) @ w_ple_gate[i])
        x = x + gate * (p[i] @ w_ple_proj[i])
    return rmsnorm(x, g_final)


def setup_inputs(seed=0):
    out = dict(first_inputs(seed))
    for name, value in second_inputs(seed + 1).items():
        if name != "x":
            out[name + "_2"] = value
    return out


def reference(
    x, c, w_ada, b_ada, norm1_g, w_in, b_gate, rel_bias, pool_w, pool_scale, w_branch_attn,
    w_branch_pool, w_out, norm2_g, w_router_group, b_router_group, w_router_expert,
    b_router_expert, w_expert_gate, w_expert_up, w_expert_down, norm_f_g, p_2, g_mix_2, w_in_2,
    lam_q1_2, lam_k1_2, lam_q2_2, lam_k2_2, g_subln_2, w_conv_2, b_conv_2, w_rg_2, b_rg_2,
    w_ig_2, b_ig_2, lru_lambda_2, w_attn_br_2, w_lru_br_2, w_out_2, g_moe_2, w_rt_group_2,
    b_rt_group_2, w_rt_expert_2, b_rt_expert_2, w_e_gate_2, w_e_up_2, w_e_down_2, g_ple_2,
    w_ple_gate_2, w_ple_proj_2, g_final_2,
):
    x = first_block(
        x, c, w_ada, b_ada, norm1_g, w_in, b_gate, rel_bias, pool_w, pool_scale, w_branch_attn,
        w_branch_pool, w_out, norm2_g, w_router_group, b_router_group, w_router_expert,
        b_router_expert, w_expert_gate, w_expert_up, w_expert_down, norm_f_g,
    )
    return second_block(
        x, p_2, g_mix_2, w_in_2, lam_q1_2, lam_k1_2, lam_q2_2, lam_k2_2, g_subln_2, w_conv_2,
        b_conv_2, w_rg_2, b_rg_2, w_ig_2, b_ig_2, lru_lambda_2, w_attn_br_2, w_lru_br_2,
        w_out_2, g_moe_2, w_rt_group_2, b_rt_group_2, w_rt_expert_2, b_rt_expert_2, w_e_gate_2,
        w_e_up_2, w_e_down_2, g_ple_2, w_ple_gate_2, w_ple_proj_2, g_final_2,
    )


_drawn_inputs = setup_inputs


def setup_inputs(seed=0):
    import zlib

    import numpy as np

    out = dict(_drawn_inputs(seed))
    spreads = {}
    factors = {'norm1_g': 3.501,
     'b_gate': 8.0,
     'b_router_group': 64.0,
     'b_router_expert': 11.591,
     'lam_q1_2': 14.945,
     'b_rg_2': 29.054,
     'b_ig_2': 8.0,
     'b_rt_group_2': 20.513,
     'b_rt_expert_2': 4.297,
     'g_ple_2': 6.898}
    for name, (base, spread) in spreads.items():
        noise = np.random.default_rng([zlib.crc32(name.encode()), seed]).standard_normal(out[name].shape)
        drawn = base * np.exp(spread * noise) if base else spread * noise
        out[name] = jnp.asarray(drawn.astype(out[name].dtype))
    for name, factor in factors.items():
        out[name] = (out[name] * factor).astype(out[name].dtype)
    return out
```

```python
from contextlib import ExitStack

import concourse.bass as bass
from concourse import mybir

ALU = mybir.AluOpType
ACT = mybir.ActivationFunctionType
AX = mybir.AxisListType
F32 = mybir.dt.float32
I32 = mybir.dt.int32

P = 128
D = 1024
T = 256
NT = T // P
DC = D // P
HEADS = 8
HD = 64
SLOT_COLS = 4096
RING = 8
EXPERTS = 32
GROUPS = 4
PER_GROUP = EXPERTS // GROUPS
PAIRS = EXPERTS // 2
CAP = 64
UNROLL = 4
ROUNDS = T // CAP
EXTRA = (2 * T - 1) // CAP
NLOG = GROUPS + EXPERTS
FAR = -1.0e30
EPS = 1e-6
EPS_SUB = 1e-5
BUCKETS = 32
WINDOWS = (2, 4, 8, 16)
LAM_INIT = 0.2
SCALE = HD ** -0.5
LRU_C = 8.0

W5 = ["u", "z0", "z1", "z2", "z3"]
STREAM1 = [f"ada{j}" for j in range(4)] + ["q", "k", "v"]
for _h in range(HEADS):
    STREAM1 += [f"ada{4 + _h}"] + (W5[_h:_h + 1])
STREAM1 += ["brA", "brP", "out0", "out1"]
STREAM2 = [f"{n}{j}_2" for n in ("q", "k", "v", "xr", "gr", "ga", "gb", "abr", "lbr", "o") for j in range(2)]
STREAM3 = ["pg0", "pg1", "pp"]
SLOTS_MOE = 3 * EXPERTS
MOE_AT = {1: len(STREAM1), 2: len(STREAM1) + SLOTS_MOE + len(STREAM2)}
SLOT = {key: n for n, key in enumerate(STREAM1)}
SLOT.update({key: MOE_AT[1] + SLOTS_MOE + n for n, key in enumerate(STREAM2)})
SLOT.update({key: MOE_AT[2] + SLOTS_MOE + n for n, key in enumerate(STREAM3)})

DENSE = [(key, g) for key in STREAM1[:-4] for g in range(1 if key[:3] == "ada" else 2)]
DENSE += [("pool", 0), ("pool", 1)]
DENSE += [(key, g) for key in ("brA", "brP") for g in range(4)]
DENSE += [(key, g) for key in ("out0", "out1") for g in range(2)]
DENSE += [(key, g) for key in STREAM2[:14] for g in range(2)]
DENSE += [("lru", c) for c in range(DC)]
DENSE += [(key, g) for key in STREAM2[14:] for g in range(2)]
DENSE += [(key, g) for key in ("pg0", "pg1") for g in range(2)] + [("pp", g) for g in range(4)]
DAT = {key: n for n, key in enumerate(DENSE)}
LAST = {key: n for n, (key, _) in enumerate(DENSE)}

SMALL = ["vecA", "vecB", "bias", "lam"] + [f"mod{j}" for j in range(4)] + ["norm1"]
SMALL += [f"mod{4 + h}" for h in range(HEADS)] + ["norm2", "logit1", "pos1", "normf", "normx"]
SMALL += [f"sub{g}" for g in range(4)] + ["normm", "logit2", "pos2", "normp", "norme"]
SAT = {key: n for n, key in enumerate(SMALL)}

TURNS = [("x", g) for g in range(4)] + [("h1", g) for g in range(4)]
TURNS += [("h2", g) for g in range(4)] + [("p", 0)] + [("y", g) for g in range(4)]
TAT = {key: n for n, key in enumerate(TURNS)}

ROWS_A = {"norm1_g": (0, 8), "b_gate": (8, 16), "pool_scale": (24, 4), "norm2_g": (28, 8),
          "norm_f_g": (36, 8), "c": (44, 8), "b_ada": (52, 48)}
ROWS_B = {"g_mix_2": (0, 8), "w_conv_2": (8, 32), "b_conv_2": (40, 8), "b_rg_2": (48, 8),
          "b_ig_2": (56, 8), "lru_lambda_2": (64, 8), "g_subln_2": (72, 1), "g_moe_2": (73, 8),
          "g_ple_2": (81, 8), "g_final_2": (89, 8)}


def build(nc, a, out):
    ctx = ExitStack()
    with ctx:
        def sb(name, shape, dt=F32):
            return ctx.enter_context(nc.sbuf_tensor(name, shape, dt))

        signals = {}

        def sig(name):
            if name not in signals:
                signals[name] = ctx.enter_context(nc.semaphore(name))
            return signals[name]

        bank = [ctx.enter_context(nc.psum_tensor(f"bank{i}", [P, 512], F32)) for i in range(8)]
        ring = sb("ring", [P, RING, SLOT_COLS])
        tile = [sb(f"tile{i}", [P, 2048]) for i in range(9)]
        att_s = sb("att_s", [P, 1024])
        att_p = sb("att_p", [P, 1024])
        att_pt = sb("att_pt", [P, 2, 256])
        mask = sb("mask", [P, 2, 256])
        ev = sb("ev", [P, 2, 512])
        ident = sb("ident", [P, P])
        ones = sb("ones", [P, P])
        tri = sb("tri", [P, P])
        vec_a = sb("vec_a", [P, P])
        vec_b = sb("vec_b", [P, P])
        c_pad = sb("c_pad", [P, DC, 32])
        mod = sb("mod", [P, 48])
        gain = sb("gain", [P, 2, DC])
        half_b = sb("half_b", [P, 16])
        w_rt = sb("w_rt", [P, DC, NLOG])
        b_rt = sb("b_rt", [1, 2, NLOG])
        desc = sb("desc", [P, 2, 8])
        iota_cap = sb("iota_cap", [P, CAP])
        inv_cnt = sb("inv_cnt", [P, 16])
        rel = sb("rel", [33, HEADS])
        lam_v = ev[0:1, 0, 0:256].rearrange("p (n d) -> p n d", n=4)
        lam_s = sb("lam_s", [1, 8])
        neg_lam = sb("neg_lam", [P, 1])
        s8 = sb("s8", [P, 8, DC])
        sub_gain = sb("sub_gain", [P, 1])
        mx = sb("mx", [P, 4])
        sm = sb("sm", [P, 4])
        rs = sb("rs", [P, 4])
        rt = att_p[:, 768:1024]
        code_of = sb("code_of", [P, (ROUNDS - 1) * EXPERTS])
        one_to = sb("one_to", [P, EXTRA])
        extra = sb("extra", [1, 2, 8], I32)

        bias_dram = nc.dram_tensor("bias_dram", [HEADS, 512], F32, kind="Internal").ap()
        bias_rows = nc.dram_tensor("bias_rows", [P, HEADS, 512], F32, kind="Internal").ap()

        def dtile(i):
            return tile[i][:, :].rearrange("p (c t) -> p c t", t=T)

        def half(i, n):
            return tile[i][:, 1024 * n:1024 * n + 1024].rearrange("p (c t) -> p c t", t=T)

        xT, hT = dtile(0), dtile(1)
        x_rows = tile[1][:, :].rearrange("p (i d) -> p i d", i=NT)
        q1, k1 = half(2, 0), half(2, 1)
        v1 = tile[3][:, 0:1024].rearrange("p (i d) -> p i d", i=NT)
        o1 = half(3, 1)
        z1 = [dtile(4), dtile(5)]
        u1, pingpong = half(6, 0), [half(6, 1), half(7, 0)]
        pool_w = tile[7][:, 1024:1536].rearrange("p (g d) -> p g d", g=4)
        pool_d, pool_y = half(8, 0), half(8, 1)
        bias_sb = [att_s[:, 512:1024], att_p[:, 512:1024]]
        q2, k2 = dtile(2), dtile(3)
        v2 = tile[4][:, :].rearrange("p (i d) -> p i d", i=NT)
        xr, gr, ga, gb = dtile(5), dtile(6), dtile(7), dtile(8)
        xc, lru_ti, lru_a = dtile(3), dtile(4), dtile(1)
        lru_w = ev[:, :, :].rearrange("p g (c v) -> p g c v", v=HD)
        sub_sq = [att_s[:, 0:512], att_s[:, 512:1024], att_p[:, 0:512], att_p[:, 512:1024]]
        sub_r = [att_pt[:, :, :].rearrange("p k t -> p (k t)"), mask[:, :, :].rearrange("p k t -> p (k t)")]
        h_rows = tile[2][:, :].rearrange("p (i d) -> p i d", i=NT)
        yacc = dtile(3)
        packed = tile[4][:, 0:1024].rearrange("p (c s) -> p c s", s=P)
        act_g, act_u = tile[5][:, 0:512], tile[5][:, 512:1024]
        act_t = tile[5][:, 1024:1536].rearrange("p (k s) -> p k s", s=P)
        spread = tile[5][:, 1536:1792]
        y_e = tile[6][:, 0:1024]
        pick = tile[6][:, 1024:1280].rearrange("p (i s) -> p i s", s=P)
        pick_w = tile[6][:, 1280:1536].rearrange("p (i s) -> p i s", s=P)
        comb = tile[8][:, 0:68].rearrange("p (i e) -> p i e", i=NT)
        posm = tile[8][:, 68:136].rearrange("p (i e) -> p i e", i=NT)
        sel = tile[8][:, 136:200].rearrange("p (i e) -> p i e", i=NT)
        ov_base = tile[8][:, 200:200 + EXTRA]
        ov_code = tile[8][:, 208:208 + EXTRA]
        ov_expert = tile[8][:, 216:216 + EXTRA]
        lg = tile[8][:, 264:336].rearrange("p (i e) -> p i e", i=NT)
        zg = tile[8][:, 336:400].rearrange("p (i g e) -> p i g e", i=NT, g=GROUPS)
        r8 = tile[8][:, 400:560].rearrange("p (n i e) -> p n i e", i=NT, e=8)
        r1 = tile[8][:, 560:584].rearrange("p (n i) -> p n i", i=NT)
        n_code = (ROUNDS - 1) * EXPERTS
        ov_hot = tile[7][:, 0:EXTRA * n_code].rearrange("p (j n) -> p j n", j=EXTRA)
        ov_more = tile[7][:, 1024:1024 + n_code]
        ov_rank = tile[7][:, 1280:1280 + n_code]
        counts = tile[7][:, 1536:1536 + EXPERTS]
        packed_1 = tile[4][:, 0:DC * CAP].rearrange("p (c s) -> p c s", s=CAP)

        def rows_of(w, n0, n1):
            return w[:, n0:n1].rearrange("(k p) n -> p k n", p=P)

        w_in, w_in2 = a["w_in"][0], a["w_in_2"][0]
        source = {}
        for j in range(12):
            source[f"ada{j}"] = rows_of(a["w_ada"][0], 512 * j, 512 * j + 512)
        for n, key in enumerate(["q", "k", "v"] + W5):
            source[key] = rows_of(w_in, 512 * n, 512 * n + 512)
        source["brA"] = rows_of(a["w_branch_attn"][0], 0, D)
        source["brP"] = rows_of(a["w_branch_pool"][0], 0, D)
        for n, key in enumerate(STREAM2[:14]):
            source[key] = rows_of(w_in2, 512 * n, 512 * n + 512)
        for j in range(2):
            source[f"out{j}"] = rows_of(a["w_out"][0], 512 * j, 512 * j + 512)
            source[f"abr{j}_2"] = rows_of(a["w_attn_br_2"][0], 512 * j, 512 * j + 512)
            source[f"lbr{j}_2"] = rows_of(a["w_lru_br_2"][0], 512 * j, 512 * j + 512)
            source[f"o{j}_2"] = rows_of(a["w_out_2"][0], 512 * j, 512 * j + 512)
            source[f"pg{j}"] = rows_of(a["w_ple_gate_2"][0], 512 * j, 512 * j + 512)
        source["pp"] = rows_of(a["w_ple_proj_2"][0], 0, D)
        expert_w = {
            1: [a["w_expert_gate"][0], a["w_expert_up"][0], a["w_expert_down"][0]],
            2: [a["w_e_gate_2"][0], a["w_e_up_2"][0], a["w_e_down_2"][0]],
        }

        def slot_view(s, kc):
            return ring[:, s, 0:kc * (1024 if kc < 8 else 512)].rearrange("p (k n) -> p k n", k=kc)

        def kc_of(key):
            return {"brA": 4, "brP": 4, "pp": 2}[key] if key in ("brA", "brP", "pp") else 8

        def expert_src(blk, which, e):
            w = expert_w[blk][which][bass.ds(e, 1)]
            return w.rearrange("a (k p) n -> p (a k) n", p=P)

        PAIR_SLOTS = [(0, 0), (0, 1), (1, 0), (1, 1), (2, 0), (2, 1)]

        block = ctx.enter_context(nc.Block())

        @block.sync
        def _(sp):
            def slot_free(n):
                m = n - RING
                if m < 0:
                    return
                if m < MOE_AT[1]:
                    sp.wait_ge(sig("dense_done"), LAST[STREAM1[m]] + 1)
                elif m < MOE_AT[1] + SLOTS_MOE:
                    pair, j = divmod(m - MOE_AT[1], 6)
                    sp.wait_ge(sig(f"pe_slots{j // 2}_1"), pair + 1)
                elif m < MOE_AT[2]:
                    sp.wait_ge(sig("dense_done"), LAST[STREAM2[m - MOE_AT[1] - SLOTS_MOE]] + 1)
                elif m < MOE_AT[2] + SLOTS_MOE:
                    pair, j = divmod(m - MOE_AT[2], 6)
                    sp.wait_ge(sig(f"pe_slots{j // 2}_2"), pair + 1)

            def load(key):
                n = SLOT[key]
                slot_free(n)
                sp.dma_start(slot_view(n % RING, kc_of(key)), source[key]).then_inc(sig(f"slot{n % RING}"), 16)

            def load_expert_slot(blk, j, e):
                n = MOE_AT[blk] + j
                which, second = PAIR_SLOTS[j % 6]
                view = slot_view(n % RING, 4 if which == 2 else 8)
                sp.dma_start(view, expert_src(blk, which, e + second)).then_inc(sig(f"slot{n % RING}"), 16)

            def experts(blk):
                for j in range(RING):
                    slot_free(MOE_AT[blk] + j)
                    load_expert_slot(blk, j, 2 * (j // 6))
                body = 6 * UNROLL
                with sp.Fori(0, PAIRS // UNROLL - 1) as it:
                    for j in range(RING, RING + body):
                        pair, k = divmod(j - RING, 6)
                        sp.wait_ge(sig(f"pe_slots{k // 2}_{blk}"), it * UNROLL + (pair + 1))
                        load_expert_slot(blk, j, it * (2 * UNROLL) + 2 * (j // 6))
                last = (PAIRS // UNROLL - 1) * body
                for j in range(last + RING, SLOTS_MOE):
                    slot_free(MOE_AT[blk] + j)
                    load_expert_slot(blk, j, 2 * (j // 6))

            def further(blk):
                sp.wait_ge(sig(f"extra_{blk}"), 1)
                count = sp.value_load(extra[0:1, blk - 1, 0:1], min_val=0, max_val=EXTRA)

                def load_turn(at):
                    e = sp.value_load(extra[0:1, blk - 1, bass.ds(at + 1, 1)], min_val=0, max_val=EXPERTS - 1)
                    for which in range(3):
                        sp.dma_start(slot_view(which, 4 if which == 2 else 8), expert_src(blk, which, e))\
                          .then_inc(sig(f"ov_slot{which}_{blk}"), 16)

                with sp.If(count > 0):
                    sp.wait_ge(sig(f"pe_slots2_{blk}"), PAIRS)
                    load_turn(0)
                    with sp.Fori(1, EXTRA) as j:
                        with sp.If(count > j):
                            sp.wait_ge(sig(f"ov_down_{blk}"), j)
                            load_turn(j)
                        with sp.Else():
                            sp.nop()
                    sp.wait_ge(sig("x_new"), {1: 5, 2: 13}[blk])
                with sp.Else():
                    sp.nop()

            for key in STREAM1:
                load(key)
            experts(1)
            further(1)
            for key in STREAM2:
                load(key)
            experts(2)
            further(2)
            for key in STREAM3:
                load(key)
            sp.wait_ge(sig("turn_out"), TAT[("y", 3)] + 1)
            sp.dma_start(out[0].rearrange("(i p) d -> p i d", p=P),
                         tile[2][:, :].rearrange("p (i d) -> p i d", i=NT)).then_inc(sig("stored"), 16)
            sp.wait_ge(sig("stored"), 16)

        @block.gpsimd
        def _(pool):
            pool.memset(att_s[:, 0:256], 0.0).then_inc(sig("rows_clear"), 1)
            pool.memset(rel[:, :], 1.0).then_inc(sig("rows_clear"), 1)
            pool.memset(c_pad[:, :, :], 0.0).then_inc(sig("pool_set"), 1)
            pool.memset(ones[:, :], 1.0).then_inc(sig("pool_set"), 1)
            pool.memset(mask[:, :, :], 0.0).then_inc(sig("pool_set"), 1)
            pool.wait_ge(sig("pool_set"), 3)
            pool.affine_select(out=ident[:, :], in_=ones[:, :], compare_op=ALU.is_equal, fill=0.0, base=0,
                               pattern=[[-1, P]], channel_multiplier=1).then_inc(sig("consts"), 1)
            pool.affine_select(out=tri[:, :], in_=ones[:, :], compare_op=ALU.is_gt, fill=0.0, base=0,
                               pattern=[[1, P]], channel_multiplier=-1).then_inc(sig("consts"), 1)
            pool.affine_select(out=mask[:, :, :], in_=mask[:, :, :], compare_op=ALU.is_ge, fill=FAR, base=0,
                               pattern=[[P, 2], [-1, T]], channel_multiplier=1).then_inc(sig("consts"), 1)
            pool.iota(desc[:, :, :], pattern=[[0, 2], [-1, 8]], base=8, channel_multiplier=0,
                      allow_small_or_imprecise_dtypes=True).then_inc(sig("consts"), 1)
            pool.iota(code_of[:, :], pattern=[[CAP, ROUNDS - 1], [1, EXPERTS]], base=CAP, channel_multiplier=0,
                      allow_small_or_imprecise_dtypes=True).then_inc(sig("consts"), 1)
            pool.iota(one_to[:, :], pattern=[[1, EXTRA]], base=1, channel_multiplier=0,
                      allow_small_or_imprecise_dtypes=True).then_inc(sig("consts"), 1)
            pool.iota(iota_cap[:, :], pattern=[[1, CAP]], base=0, channel_multiplier=0,
                      allow_small_or_imprecise_dtypes=True).then_inc(sig("consts"), 1)
            pool.iota(inv_cnt[:, :], pattern=[[1, 16]], base=1, channel_multiplier=0,
                      allow_small_or_imprecise_dtypes=True).then_inc(sig("consts"), 1)

        CONSTS = 8

        @block.tensor
        def _(pe):
            small_n, dense_n, turn_n = [0], [0], [0]

            def small_bank(key):
                assert SAT[key] == small_n[0], key
                if small_n[0]:
                    pe.wait_ge(sig("small_read"), small_n[0])
                small_n[0] += 1
                return bank[7]

            def dense_bank(key, g):
                n = dense_n[0]
                assert DAT[(key, g)] == n, (key, g)
                if n >= 2:
                    pe.wait_ge(sig("dense_out"), n - 1)
                dense_n[0] += 1
                return bank[n % 2]

            def turn(key, sources):
                n = turn_n[0]
                assert TAT[key] == n, key
                if n >= 2:
                    pe.wait_ge(sig("turn_out"), n - 1)
                for j, src in enumerate(sources):
                    mm = pe.transpose(bank[2 + n % 2][:, j * P:(j + 1) * P], src, ident[:, :])
                mm.then_inc(sig("turned"), 1)
                turn_n[0] += 1

            def slot(key):
                n = SLOT[key]
                pe.wait_ge(sig(f"slot{n % RING}"), 16 * (n // RING + 1))
                return slot_view(n % RING, kc_of(key))

            def project(key, rhs, groups=2, ready=None):
                w = slot(key)
                kc = kc_of(key)
                for g in range(groups):
                    b = dense_bank(key, g)
                    for j in range(2):
                        n0 = (2 * g + j) * P
                        for k in range(kc):
                            if ready and g == 0 and j == 0:
                                pe.wait_ge(sig(ready[0]), ready[1] + k + 1)
                            mm = pe.matmul(b[:, j * T:(j + 1) * T], w[:, k, n0:n0 + P], rhs[:, k, :],
                                           start=(k == 0), stop=(k == kc - 1))
                    mm.then_inc(sig("dense_done"), 1)

            def project_rows(key, lhs):
                w = slot(key)
                for i in range(NT):
                    b = dense_bank(key, i)
                    for k in range(DC):
                        mm = pe.matmul(b[:, :], lhs[:, k, i * P:(i + 1) * P], w[:, k, :],
                                       start=(k == 0), stop=(k == DC - 1))
                    mm.then_inc(sig("dense_done"), 1)

            def ada(j):
                w = slot(f"ada{j}")
                b = dense_bank(f"ada{j}", 0)
                for k in range(DC):
                    r = 32 * (k % 4)
                    mm = pe.matmul(b[r:r + 32, :], c_pad[:, k, :], w[:, k, :], start=(k < 4), stop=(k >= 4))
                mm.then_inc(sig("dense_done"), 1)

            def ada_cols(j):
                b = small_bank(f"mod{j}")
                pe.wait_ge(sig("dense_out"), DAT[(f"ada{j}", 0)] + 1)
                for m in range(4):
                    mm = pe.matmul(b[:, m:m + 1], ev[:, j % 2, m * P:(m + 1) * P], ones[:, 0:1],
                                   start=True, stop=True)
                mm.then_inc(sig("small_done"), 1)

            def norm_sum(name, n_done):
                b = small_bank(name)
                for c in range(DC):
                    if c % 2 == 0:
                        pe.wait_ge(sig("squares"), 4 * n_done + c // 2 + 1)
                    mm = pe.matmul(b[:, 0:T], ones[:, :], hT[:, c, :], start=(c == 0), stop=(c == DC - 1))
                mm.then_inc(sig("small_done"), 1)

            pe.wait_ge(sig("consts"), CONSTS)
            for n, key in enumerate(("vecA", "vecB")):
                b = small_bank(key)
                pe.wait_ge(sig(f"{key}_in"), 16 * len(ROWS_A if n == 0 else ROWS_B))
                pe.transpose(b[:, 0:P], att_s[:, n * P:(n + 1) * P], ident[:, :]).then_inc(sig("small_done"), 1)
            b = small_bank("bias")
            pe.wait_ge(sig("bucket_in"), 16)
            pe.wait_ge(sig("rel_in"), 16)
            pe.matmul(b[0:HEADS, :], rel[:, :], att_s[0:33, 512:1024], start=True, stop=True)\
              .then_inc(sig("small_done"), 1)
            b = small_bank("lam")
            pe.wait_ge(sig("lam_ready"), 1)
            pe.matmul(b[:, 0:1], ones[0:1, :], lam_s[0:1, 4:5], start=True, stop=True).then_inc(sig("small_done"), 1)
            pe.wait_ge(sig("x_in"), 16)
            for g in range(4):
                turn(("x", g), [x_rows[:, i, (2 * g + c) * P:(2 * g + c + 1) * P] for c in range(2) for i in range(NT)])
            pe.wait_ge(sig("c_ready"), 1)
            for j in range(4):
                ada(j)
                ada_cols(j)
            norm_sum("norm1", 0)
            project("q", hT, ready=("h_shifted", 0))
            project("k", hT)
            project_rows("v", hT)

            def scores_1(h):
                r, c = HD * (h % 2), h // 2
                if h == 0:
                    pe.wait_ge(sig("dense_out"), LAST["k"] + 1)
                if h >= 2:
                    pe.wait_ge(sig("scores_read"), h - 1)
                for i in range(NT):
                    mm = pe.matmul(bank[2 + h % 2][:, i * T:(i + 1) * T], q1[r:r + HD, c, i * P:(i + 1) * P],
                                   k1[r:r + HD, c, :], start=True, stop=True)
                mm.then_inc(sig("scores"), 1)

            def turn_probs(h):
                pe.wait_ge(sig("probs"), h + 1)
                if h:
                    pe.wait_ge(sig("probs_t"), h)
                for kt in range(2):
                    for i in range(NT):
                        mm = pe.transpose(bank[4][:, kt * T + i * P:kt * T + (i + 1) * P],
                                          att_p[:, i * T + kt * P:i * T + (kt + 1) * P], ident[:, :])
                mm.then_inc(sig("probs_turned"), 1)
                pe.wait_ge(sig("probs_t"), h + 1)

            def values_1(h):
                turn_probs(h)
                if h == 0:
                    pe.wait_ge(sig("dense_out"), LAST["v"] + 1)
                if h % 2 == 0 and h >= 4:
                    pe.wait_ge(sig("o_out"), h // 2 - 1)
                r = HD * (h % 2)
                for kt in range(2):
                    mm = pe.matmul(bank[5 + (h // 2) % 2][r:r + HD, 0:T], v1[:, kt, h * HD:(h + 1) * HD],
                                   att_pt[:, kt, :], start=(kt == 0), stop=(kt == 1))
                if h % 2:
                    mm.then_inc(sig("o_done"), 1)

            for h in range(HEADS):
                ada(4 + h)
                if h < len(W5):
                    project(W5[h], hT)
                ada_cols(4 + h)
                scores_1(h)
                if h:
                    values_1(h - 1)
            values_1(HEADS - 1)
            for g in range(2):
                b = dense_bank("pool", g)
                pe.wait_ge(sig("pool_parts"), 2 * g + 2)
                if g == 0:
                    pe.wait_ge(sig("pool_w_in"), 16)
                for j in range(2):
                    mm = pe.matmul(b[:, j * T:(j + 1) * T], pool_w[:, 2 * g + j, :], pool_d[:, 2 * g + j, :],
                                   start=True, stop=True)
                mm.then_inc(sig("dense_done"), 1)
            pe.wait_ge(sig("o_out"), HEADS // 2)
            project("brA", o1, groups=4)
            pe.wait_ge(sig("dense_out"), LAST["pool"] + 1)
            project("brP", pool_y, groups=4)
            pe.wait_ge(sig("mixed"), 4)
            project("out0", z1[0])
            project("out1", z1[0])

            def route(blk, normed, count):
                for g in range(4):
                    if g == 0:
                        pe.wait_ge(sig(normed), count)
                    turn((f"h{blk}", g), [hT[:, 4 * (g % 2) + c, (g // 2) * P:(g // 2 + 1) * P] for c in range(4)])
                b = small_bank(f"logit{blk}")
                pe.wait_ge(sig("w_rt_in"), {1: 2 * 16, 2: (3 + GROUPS) * 16}[blk])
                pe.wait_ge(sig("b_rt_in"), 64)
                for i in range(NT):
                    for k in range(DC):
                        pe.matmul(b[:, i * NLOG:(i + 1) * NLOG], hT[:, k, i * P:(i + 1) * P], w_rt[:, k, :],
                                  start=(k == 0), stop=False)
                    mm = pe.matmul(b[:, i * NLOG:(i + 1) * NLOG], ones[0:1, :], b_rt[0:1, blk - 1, :],
                                   start=False, stop=True)
                mm.then_inc(sig("small_done"), 1)
                b = small_bank(f"pos{blk}")
                pe.wait_ge(sig("sel_ready"), blk)
                pe.matmul(b[:, 0:EXPERTS], tri[:, :], sel[:, 0, :], start=True, stop=True)
                pe.matmul(b[:, EXPERTS:2 * EXPERTS], tri[:, :], sel[:, 1, :], start=True, stop=False)
                pe.matmul(b[:, EXPERTS:2 * EXPERTS], ones[:, :], sel[:, 0, :], start=False, stop=True)
                pe.matmul(b[:, 2 * EXPERTS:3 * EXPERTS], ones[:, :], sel[:, 0, :], start=True, stop=False)
                pe.matmul(b[:, 2 * EXPERTS:3 * EXPERTS], ones[:, :], sel[:, 1, :], start=False, stop=True)\
                  .then_inc(sig("small_done"), 1)
                pe.wait_ge(sig("turn_out"), TAT[(f"h{blk}", 3)] + 1)

            def gather(blk):
                for c in range(DC):
                    for i in range(NT):
                        mm = pe.matmul(bank[4 + c // 4][:, (c % 4) * P:(c % 4 + 1) * P],
                                       h_rows[:, i, c * P:(c + 1) * P], pick[:, i, :],
                                       start=(i == 0), stop=(i == NT - 1))
                    if c % 4 == 3:
                        mm.then_inc(sig(f"gathered_{blk}"), 1)

            def experts(blk):
                pe.wait_ge(sig(f"picks_{blk}"), 1)
                gather(blk)
                body = 6 * UNROLL
                with pe.Fori(0, PAIRS // UNROLL) as it:
                    for u in range(UNROLL):
                        at = it * UNROLL + u

                        def weights(which):
                            views = []
                            for second in range(2):
                                n = MOE_AT[blk] + 6 * u + 2 * which + second
                                pe.wait_ge(sig(f"slot{n % RING}"), it * (16 * body // RING) + 16 * (n // RING + 1))
                                views.append(slot_view(n % RING, 4 if which == 2 else 8))
                            return views

                        pe.wait_ge(sig(f"packed_{blk}"), at * 2 + 2)
                        for which, b in ((0, bank[0]), (1, bank[1])):
                            w = weights(which)
                            for k in range(DC):
                                for second in range(2):
                                    r = CAP * second
                                    mm = pe.matmul(b[r:r + CAP, :], packed[:, k, r:r + CAP], w[second][:, k, :],
                                                   start=(k == 0), stop=(k == DC - 1))
                            mm.then_inc(sig(f"pe_slots{which}_{blk}"), 1)
                        pe.wait_ge(sig(f"summed_{blk}"), at * 4 + 1)
                        for i in range(NT):
                            mm = pe.transpose(bank[7][:, i * P:(i + 1) * P], pick_w[:, i, :], ident[:, :])
                        mm.then_inc(sig(f"spread_turned_{blk}"), 1)
                        pe.wait_ge(sig(f"acts_{blk}"), at + 1)
                        for k in range(4):
                            mm = pe.transpose(bank[6][:, k * P:(k + 1) * P], act_u[:, k * P:(k + 1) * P], ident[:, :])
                        mm.then_inc(sig(f"acts_turned_{blk}"), 1)
                        w = weights(2)
                        pe.wait_ge(sig(f"acts_t_{blk}"), at + 1)
                        for n in range(2):
                            for k in range(4):
                                for second in range(2):
                                    r = CAP * second
                                    mm = pe.matmul(bank[2 + n][r:r + CAP, :], act_t[:, k, r:r + CAP],
                                                   w[second][:, k, n * 512:(n + 1) * 512],
                                                   start=(k == 0), stop=(k == 3))
                            mm.then_inc(sig(f"pe_slots2_{blk}" if n else f"down0_{blk}"), 1)
                        pe.wait_ge(sig(f"picks_{blk}"), at + 2)
                        gather(blk)
                        pe.wait_ge(sig(f"spread_{blk}"), at + 1)
                        pe.wait_ge(sig(f"y_e_{blk}"), at * 2 + 2)
                        for q in range(4):
                            if q >= 2:
                                pe.wait_ge(sig(f"summed_{blk}"), at * 4 + q)
                            for j in range(2):
                                c = 2 * q + j
                                mm = pe.matmul(bank[6 + q % 2][:, j * T:(j + 1) * T], y_e[:, c * P:(c + 1) * P],
                                               spread, start=True, stop=True)
                            mm.then_inc(sig(f"scattered_{blk}"), 1)

            def further(blk):
                pe.wait_ge(sig(f"extra_{blk}"), 1)
                count = pe.value_load(extra[0:1, blk - 1, 0:1], min_val=0, max_val=EXTRA)
                with pe.If(count > 0):
                    pe.wait_ge(sig(f"summed_{blk}"), 4 * PAIRS + 1)
                    pe.wait_ge(sig(f"packed_{blk}"), 2 * PAIRS + 2)
                    with pe.Fori(0, EXTRA) as j:
                        with pe.If(count > j):
                            further_turn(blk, j)
                        with pe.Else():
                            pe.nop()
                with pe.Else():
                    pe.nop()

            def further_turn(blk, j):
                pe.wait_ge(sig(f"ov_picks_{blk}"), j + 1)
                for c in range(DC):
                    for i in range(NT):
                        mm = pe.matmul(bank[4][:, c * CAP:(c + 1) * CAP], h_rows[:, i, c * P:(c + 1) * P],
                                       pick[:, i, 0:CAP], start=(i == 0), stop=(i == NT - 1))
                mm.then_inc(sig(f"ov_gathered_{blk}"), 1)
                for i in range(NT):
                    mm = pe.transpose(bank[7][:, i * P:(i + 1) * P], pick_w[:, i, :], ident[:, :])
                mm.then_inc(sig(f"ov_spread_turned_{blk}"), 1)
                pe.wait_ge(sig(f"ov_packed_{blk}"), j + 1)
                for which in range(2):
                    pe.wait_ge(sig(f"ov_slot{which}_{blk}"), j * 16 + 16)
                    w = slot_view(which, 8)
                    for k in range(DC):
                        for part in range(2):
                            mm = pe.matmul(bank[which][CAP * part:CAP * part + CAP, 0:256], packed_1[:, k, :],
                                           w[:, k, 256 * part:256 * part + 256], start=(k == 0), stop=(k == DC - 1))
                mm.then_inc(sig(f"ov_gu_{blk}"), 1)
                pe.wait_ge(sig(f"ov_acts_{blk}"), j + 1)
                for m in range(2):
                    mm = pe.transpose(bank[6][:, m * P:(m + 1) * P], act_u[:, m * P:(m + 1) * P], ident[:, :])
                mm.then_inc(sig(f"ov_turned_{blk}"), 1)
                pe.wait_ge(sig(f"ov_slot2_{blk}"), j * 16 + 16)
                pe.wait_ge(sig(f"ov_acts_t_{blk}"), j + 1)
                w = slot_view(2, 4)
                for k in range(4):
                    for part in range(2):
                        mm = pe.matmul(bank[2][CAP * part:CAP * part + CAP, :],
                                       act_t[:, k % 2, CAP * (k // 2):CAP * (k // 2) + CAP],
                                       w[:, k, 512 * part:512 * part + 512], start=(k == 0), stop=(k == 3))
                mm.then_inc(sig(f"ov_down_{blk}"), 1)
                pe.wait_ge(sig(f"ov_spread_{blk}"), j + 1)
                pe.wait_ge(sig(f"ov_y_e_{blk}"), j + 1)
                for q in range(4):
                    if q >= 2:
                        pe.wait_ge(sig(f"ov_summed_{blk}"), j * 4 + (q - 1))
                    part = q // 2
                    rows = slice(CAP * part, CAP * part + CAP)
                    for m in range(2):
                        c = 2 * (q % 2) + m
                        mm = pe.matmul(bank[6 + q % 2][:, m * T:(m + 1) * T], y_e[rows, c * P:(c + 1) * P],
                                       spread[rows, :], start=True, stop=True)
                    mm.then_inc(sig(f"ov_scattered_{blk}"), 1)

            norm_sum("norm2", 1)
            route(1, "h_shifted", 2 * DC)
            experts(1)
            further(1)
            norm_sum("normf", 2)
            norm_sum("normx", 3)

            for key in STREAM2[:4]:
                project(key, hT, ready=("scaled", 3 * DC) if key == "q0_2" else None)
            project_rows("v0_2", hT)
            project_rows("v1_2", hT)

            def scores_2(h):
                if h == 0:
                    pe.wait_ge(sig("dense_out"), LAST["k1_2"] + 1)
                pe.wait_ge(sig("scores_read"), HEADS + h)
                for c in range(2):
                    for i in range(NT):
                        mm = pe.matmul(bank[2 + c][:, i * T:(i + 1) * T], q2[HD * c:HD * c + HD, h, i * P:(i + 1) * P],
                                       k2[HD * c:HD * c + HD, h, :], start=True, stop=True)
                mm.then_inc(sig("scores"), 1)

            def values_2(h):
                turn_probs(HEADS + h)
                if h == 0:
                    pe.wait_ge(sig("dense_out"), LAST["v1_2"] + 1)
                if h >= 2:
                    pe.wait_ge(sig("o_out"), HEADS // 2 + h - 1)
                for kt in range(2):
                    mm = pe.matmul(bank[5 + h % 2][:, 0:T], v2[:, kt, h * P:(h + 1) * P], att_pt[:, kt, :],
                                   start=(kt == 0), stop=(kt == 1))
                mm.then_inc(sig("o_done"), 1)

            for h in range(HEADS):
                project(STREAM2[6 + h], hT)
                scores_2(h)
                if h:
                    values_2(h - 1)
            values_2(HEADS - 1)
            for c in range(DC):
                b = dense_bank("lru", c)
                if c == 0:
                    pe.wait_ge(sig("lru_w_in"), 64)
                pe.wait_ge(sig("conv"), c + 1)
                for g in range(2):
                    for r in (0, HD):
                        mm = pe.matmul(b[r:r + HD, g * T:(g + 1) * T], lru_w[r:r + HD, g, c, :], xc[r:r + HD, c, :],
                                       start=True, stop=True)
                mm.then_inc(sig("dense_done"), 1)
            for g in range(4):
                b = small_bank(f"sub{g}")
                pe.wait_ge(sig("sub_squares"), g + 1)
                pe.matmul(b[:, :], ones[:, :], sub_sq[g], start=True, stop=True).then_inc(sig("small_done"), 1)
            pe.wait_ge(sig("o_normed"), 4)
            project("abr0_2", q2)
            project("abr1_2", q2)
            pe.wait_ge(sig("lru_y"), 1)
            project("lbr0_2", hT)
            project("lbr1_2", hT)
            pe.wait_ge(sig("mixed"), 8)
            project("o0_2", ga)
            project("o1_2", ga)
            norm_sum("normm", 4)
            route(2, "scaled", 5 * DC)
            experts(2)
            further(2)
            norm_sum("normp", 5)
            pe.wait_ge(sig("p_in"), 16)
            turn(("p", 0), [att_s[:, i * T + k * P:i * T + (k + 1) * P] for k in range(2) for i in range(NT)])
            project("pg0", hT, ready=("scaled", 5 * DC))
            project("pg1", hT)
            pe.wait_ge(sig("turn_out"), TAT[("p", 0)] + 1)
            project("pp", att_p[:, 0:512].rearrange("p (k t) -> p k t", k=2), groups=4)
            norm_sum("norme", 6)
            for g in range(4):
                if g == 0:
                    pe.wait_ge(sig("scaled"), 7 * DC)
                turn(("y", g), [hT[:, 4 * (g % 2) + c, (g // 2) * P:(g // 2 + 1) * P] for c in range(4)])

        @block.scalar
        def _(act):
            n_dense, n_root = [0], [0]

            def row_source(key):
                ap = a[key]
                if len(ap.shape) == 1:
                    return ap.rearrange("(r p) -> r p", p=P)
                if len(ap.shape) == 2:
                    return ap.rearrange("a (r p) -> (a r) p", p=P)
                if key == "w_conv_2":
                    return ap.rearrange("a j (r p) -> (a j r) p", p=P)
                return ap.rearrange("a (r s) w -> (a r) (s w)", s=2)

            act.wait_ge(sig("rows_clear"), 2)
            act.dma_start(x_rows, a["x"][0].rearrange("(i p) d -> p i d", p=P)).then_inc(sig("x_in"), 16)
            for rows, col, name in ((ROWS_A, 0, "vecA_in"), (ROWS_B, P, "vecB_in")):
                for key, (r, n) in rows.items():
                    act.dma_start(att_s[r:r + n, col:col + P], row_source(key)).then_inc(sig(name), 16)
            act.dma_start(att_s[0:33, 512:1024], a["bucket_rows"]).then_inc(sig("bucket_in"), 16)
            act.dma_start(rel[0:BUCKETS, :], a["rel_bias"]).then_inc(sig("rel_in"), 16)
            for n, key in enumerate(("lam_q1_2", "lam_k1_2", "lam_q2_2", "lam_k2_2")):
                act.dma_start(lam_v[0:1, n, :], a[key]).then_inc(sig("lam_in"), 16)
            act.dma_start(pool_w, a["pool_w"][0].rearrange("g c d -> c g d")).then_inc(sig("pool_w_in"), 16)
            act.dma_start(w_rt[:, :, 0:GROUPS], a["w_router_group"][0].rearrange("(k p) g -> p k g", p=P))\
               .then_inc(sig("w_rt_in"), 16)
            act.dma_start(w_rt[:, :, GROUPS:], a["w_router_expert"][0].rearrange("(k p) g -> p k g", p=P))\
               .then_inc(sig("w_rt_in"), 16)
            act.dma_start(b_rt[0:1, 0, 0:GROUPS], a["b_router_group"]).then_inc(sig("b_rt_in"), 16)
            act.dma_start(b_rt[0:1, 0, GROUPS:], a["b_router_expert"]).then_inc(sig("b_rt_in"), 16)
            act.dma_start(b_rt[0:1, 1, 0:GROUPS], a["b_rt_group_2"]).then_inc(sig("b_rt_in"), 16)
            act.dma_start(b_rt[0:1, 1, GROUPS:], a["b_rt_expert_2"].rearrange("a g e -> a (g e)"))\
               .then_inc(sig("b_rt_in"), 16)

            def dense_ready(key, g):
                n = n_dense[0]
                assert DAT[(key, g)] == n, (key, g)
                act.wait_ge(sig("dense_done"), n + 1)
                n_dense[0] += 1
                return bank[n % 2]

            def take(key, g, dst, func=ACT.Copy, scale=1.0):
                b = dense_ready(key, g)
                act.activation(dst, b[:, :], func, scale=scale).then_inc(sig("dense_out"), 1)

            def take_biased(key, g, dst, func, bias, scale=1.0):
                b = dense_ready(key, g)
                for j in range(2):
                    ins = act.activation(dst[j], b[:, j * T:(j + 1) * T], func, bias=bias[j], scale=scale)
                ins.then_inc(sig("dense_out"), 1)

            def take_tile(key, tile_n, at, groups=2, func=ACT.Copy, scale=1.0):
                for g in range(groups):
                    take(key, g, tile[tile_n][:, (at + 2 * g) * T:(at + 2 * g + 2) * T], func, scale)

            def squares(sem, base, step):
                for q in range(4):
                    act.wait_ge(sig(sem), base + step * (q + 1))
                    act.activation(tile[1][:, q * 512:(q + 1) * 512], tile[0][:, q * 512:(q + 1) * 512],
                                   ACT.Square).then_inc(sig("squares"), 1)

            def root(name):
                act.wait_ge(sig("small_read"), SAT[name] + 1)
                act.activation(rt[:, :], rt[:, :], ACT.Sqrt).then_inc(sig("roots"), 1)

            def shift(cols, base):
                for c in range(DC):
                    act.wait_ge(sig("scaled"), base + c + 1)
                    act.activation(hT[:, c, :], hT[:, c, :], ACT.Identity, bias=mod[:, cols + c:cols + c + 1],
                                   scale=1.0).then_inc(sig("h_shifted"), 1)

            act.wait_ge(sig("small_read"), SAT["vecA"] + 1)
            act.wait_ge(sig("pool_set"), 3)
            r = ROWS_A["c"][0]
            act.activation(c_pad[:, :, 0], vec_a[:, r:r + DC], ACT.Silu).then_inc(sig("c_ready"), 1)
            act.wait_ge(sig("lam_sums"), 1)
            act.activation(lam_s[0:1, 2:4], lam_s[0:1, 0:2], ACT.Exp).then_inc(sig("lam_exps"), 1)
            act.wait_ge(sig("lru_abs"), 1)
            act.activation(s8[:, 1, :], s8[:, 0, :], ACT.Exp, scale=-1.0).then_inc(sig("lru_exp"), 1)
            act.wait_ge(sig("small_read"), SAT["bias"] + 1)
            act.dma_start(bias_dram, att_p[0:HEADS, 0:512]).then_inc(sig("bias_stored"), 16)
            act.wait_ge(sig("turned"), TAT[("x", 3)] + 1)
            squares("turn_out", TAT[("x", 0)], 1)
            for j in range(4):
                if j >= 2:
                    act.wait_ge(sig("small_done"), SAT[f"mod{j - 2}"] + 1)
                take(f"ada{j}", 0, ev[:, j % 2, :])
            root("norm1")
            shift(0, 0)
            take_tile("q", 2, 0)
            take_tile("k", 2, 4)
            for i in range(NT):
                take("v", i, v1[:, i, :])
            act.wait_ge(sig("bias_stored"), 16)
            act.dma_start(bias_rows, bias_dram.partition_broadcast(P)).then_inc(sig("bias_copied"), 16)
            act.wait_ge(sig("bias_copied"), 16)

            def load_bias(h):
                if h >= 2:
                    act.wait_ge(sig("scores_read"), h - 1)
                for i in range(NT):
                    src = bass.AP(tensor=bias_rows.tensor, offset=512 * h + T - 1 - P * i,
                                  ap=[[HEADS * 512 - 1, P], [1, T]])
                    act.dma_start(bias_sb[h % 2][:, i * T:(i + 1) * T], src).then_inc(sig(f"bias_in{h % 2}"), 16)

            def exps(n, count):
                act.wait_ge(sig("maxima"), n + 1)
                if n:
                    act.wait_ge(sig("probs_turned"), n)
                for i in range(count):
                    ins = act.activation(att_p[:, i * T:(i + 1) * T], att_s[:, i * T:(i + 1) * T], ACT.Exp,
                                         bias=mx[:, i:i + 1], scale=1.0, accum_out=sm[:, i:i + 1])
                ins.then_inc(sig("exps"), 1)

            def probs_out(n):
                act.wait_ge(sig("probs_turned"), n + 1)
                act.activation(att_pt[:, :, :], bank[4][:, :].rearrange("p (k t) -> p k t", k=2), ACT.Copy)\
                   .then_inc(sig("probs_t"), 1)

            def o_out_1(j):
                act.wait_ge(sig("o_done"), j + 1)
                act.activation(o1[:, j, :], bank[5 + j % 2][:, 0:T], ACT.Copy).then_inc(sig("o_out"), 1)

            load_bias(0)
            for h in range(HEADS):
                j = 4 + h
                act.wait_ge(sig("small_done"), SAT[f"mod{j - 2}"] + 1)
                take(f"ada{j}", 0, ev[:, j % 2, :])
                if h == 0:
                    take_tile("u", 6, 0)
                elif h < len(W5):
                    n = h - 1
                    for g in range(2):
                        c = 4 * (n % 2) + 2 * g
                        take_biased(W5[h], g, [z1[n // 2][:, c + e, :] for e in range(2)], ACT.Tanh, scale=0.5,
                                    bias=[half_b[:, 4 * n + 2 * g + e:4 * n + 2 * g + e + 1] for e in range(2)])
                if h + 1 < HEADS:
                    load_bias(h + 1)
                if h:
                    probs_out(h - 1)
                    if h % 2 == 0:
                        o_out_1(h // 2 - 1)
                exps(h, 2)
            probs_out(HEADS - 1)
            o_out_1(HEADS // 2 - 1)
            act.wait_ge(sig("small_done"), SAT["mod11"] + 1)
            for g, key in enumerate(("w_rg_2", "w_ig_2")):
                for r in range(2):
                    act.dma_start(lru_w[HD * r:HD * r + HD, g, :, :],
                                  a[key][0].rearrange("(c r) w v -> r w c v", r=2)[r]).then_inc(sig("lru_w_in"), 16)
            r = ROWS_A["pool_scale"][0]
            for g in range(2):
                b = dense_ready("pool", g)
                for j in range(2):
                    c = 2 * g + j
                    ins = act.activation(pool_y[:, c, :], b[:, j * T:(j + 1) * T], ACT.Copy,
                                         scale=vec_a[:, r + c:r + c + 1])
                ins.then_inc(sig("dense_out"), 1)
            take_tile("brA", 1, 0, groups=4, scale=0.5)
            take_tile("brP", 2, 0, groups=4, scale=0.5)
            take_tile("out0", 6, 0)
            take_tile("out1", 6, 4)

            def experts(blk):
                def hand_on_packed(n):
                    for c in range(2):
                        act.wait_ge(sig(f"gathered_{blk}"), n * 2 + (c + 1))
                        act.activation(tile[4][:, c * 512:(c + 1) * 512], bank[4 + c][:, :], ACT.Copy)\
                           .then_inc(sig(f"packed_{blk}"), 1)

                hand_on_packed(0)
                with act.Fori(0, PAIRS // UNROLL) as it:
                    for u in range(UNROLL):
                        at = it * UNROLL + u
                        act.wait_ge(sig(f"pe_slots0_{blk}"), at + 1)
                        act.activation(act_g, bank[0][:, :], ACT.Silu).then_inc(sig(f"silu_{blk}"), 1)
                        act.wait_ge(sig(f"acts_turned_{blk}"), at + 1)
                        act.activation(tile[5][:, 1024:1536], bank[6][:, :], ACT.Copy)\
                           .then_inc(sig(f"acts_t_{blk}"), 1)
                        for n in range(2):
                            act.wait_ge(sig(f"pe_slots2_{blk}" if n else f"down0_{blk}"), at + 1)
                            act.activation(y_e[:, n * 512:(n + 1) * 512], bank[2 + n][:, :], ACT.Copy)\
                               .then_inc(sig(f"y_e_{blk}"), 1)
                        hand_on_packed(at + 1)

            def further(blk):
                act.wait_ge(sig(f"extra_{blk}"), 1)
                count = act.value_load(extra[0:1, blk - 1, 0:1], min_val=0, max_val=EXTRA)
                with act.If(count > 0):
                    with act.Fori(0, EXTRA) as j:
                        with act.If(count > j):
                            act.wait_ge(sig(f"ov_gathered_{blk}"), j + 1)
                            act.activation(tile[4][:, 0:512], bank[4][:, :], ACT.Copy).then_inc(sig(f"ov_packed_{blk}"), 1)
                            act.wait_ge(sig(f"ov_gu_{blk}"), j + 1)
                            act.activation(act_g[:, 0:256], bank[0][:, 0:256], ACT.Silu)\
                               .then_inc(sig(f"ov_silu_{blk}"), 1)
                            act.wait_ge(sig(f"ov_turned_{blk}"), j + 1)
                            act.activation(tile[5][:, 1024:1280], bank[6][:, 0:256], ACT.Copy)\
                               .then_inc(sig(f"ov_acts_t_{blk}"), 1)
                            act.wait_ge(sig(f"ov_down_{blk}"), j + 1)
                            act.activation(y_e[:, 0:512], bank[2][:, :], ACT.Copy).then_inc(sig(f"ov_y_e_{blk}"), 1)
                        with act.Else():
                            act.nop()
                with act.Else():
                    act.nop()

            def router_exps(blk):
                act.wait_ge(sig("group_gaps"), blk)
                act.activation(r8[:, 0, :, 0:4], r8[:, 1, :, 0:4], ACT.Exp).then_inc(sig("group_exps"), 1)
                act.wait_ge(sig("pair_gaps"), blk)
                act.activation(r1[:, 6, :], r1[:, 5, :], ACT.Exp).then_inc(sig("pair_exps"), 1)

            squares("x_new", 0, 1)
            root("norm2")
            shift(24, DC)
            router_exps(1)
            experts(1)
            act.dma_start(w_rt[:, :, 0:GROUPS], a["w_rt_group_2"][0].rearrange("(k p) g -> p k g", p=P))\
               .then_inc(sig("w_rt_in"), 16)
            for g in range(GROUPS):
                act.dma_start(w_rt[:, :, GROUPS + g * PER_GROUP:GROUPS + (g + 1) * PER_GROUP],
                              a["w_rt_expert_2"][0, g].rearrange("(k p) e -> p k e", p=P)).then_inc(sig("w_rt_in"), 16)
            further(1)
            squares("x_new", 4, 1)
            root("normf")
            squares("scaled", 2 * DC, 2)
            root("normx")
            for n, key in enumerate(STREAM2[:4]):
                take_tile(key, 2 + n // 2, 4 * (n % 2))
            for n in range(2):
                for i in range(NT):
                    take(f"v{n}_2", i, v2[:, i, n * 512:(n + 1) * 512])

            def o_out_2(h):
                act.wait_ge(sig("o_done"), HEADS // 2 + h + 1)
                act.activation(q2[:, h, :], bank[5 + h % 2][:, 0:T], ACT.Copy).then_inc(sig("o_out"), 1)

            for h in range(HEADS):
                func, scale = (ACT.Copy, 1.0) if h < 4 else (ACT.Tanh, 0.5)
                take_tile(STREAM2[6 + h], 5 + h // 2, 4 * (h % 2), func=func, scale=scale)
                if h:
                    probs_out(HEADS + h - 1)
                    if h >= 2:
                        o_out_2(h - 2)
                exps(HEADS + h, 4)
            probs_out(2 * HEADS - 1)
            o_out_2(HEADS - 2)
            o_out_2(HEADS - 1)
            for c in range(DC):
                b = dense_ready("lru", c)
                act.activation(xr[:, c, :], b[:, 0:T], ACT.Tanh, bias=s8[:, 3, c:c + 1], scale=0.5)\
                   .then_inc(sig("lru_r"), 1)
                act.activation(lru_ti[:, c, :], b[:, T:2 * T], ACT.Tanh, bias=s8[:, 4, c:c + 1], scale=0.5)\
                   .then_inc(sig("dense_out"), 1)
            act.wait_ge(sig("o_out"), HEADS // 2 + HEADS)
            for g in range(4):
                act.activation(sub_sq[g], tile[2][:, g * 512:(g + 1) * 512], ACT.Square).then_inc(sig("sub_squares"), 1)
            for g in range(4):
                act.wait_ge(sig("small_read"), SAT[f"sub{g}"] + 1)
                act.activation(sub_r[g % 2], sub_r[g % 2], ACT.Sqrt).then_inc(sig("sub_roots"), 1)
            act.wait_ge(sig("lru_r"), DC)
            for c in range(DC):
                act.activation(lru_a[:, c, :], xr[:, c, :], ACT.Exp, bias=s8[:, 6, c:c + 1], scale=s8[:, 6, c:c + 1])\
                   .then_inc(sig("lru_a"), 1)
            for c in range(DC):
                act.activation(xr[:, c, :], xr[:, c, :], ACT.Tanh, bias=s8[:, 5, c:c + 1], scale=s8[:, 5, c:c + 1])\
                   .then_inc(sig("lru_t"), 1)

            def take_branch(n):
                key, g = STREAM2[14 + n // 2], n % 2
                if n >= 2:
                    act.wait_ge(sig("branch_read"), n - 1)
                take(key, g, ev[:, n % 2, :], scale=0.5)

            take_branch(0)
            act.activation(tile[6][:, :], tile[6][:, :], ACT.Gelu_apprx_tanh).then_inc(sig("gelu"), 1)
            for n in range(2):
                act.wait_ge(sig("lru_frac"), n + 1)
                act.activation(tile[5][:, n * 1024:(n + 1) * 1024], tile[5][:, n * 1024:(n + 1) * 1024], ACT.Sqrt)\
                   .then_inc(sig("lru_mult"), 1)
            for n in range(1, 8):
                take_branch(n)
            act.dma_start(att_s[:, 0:512].rearrange("p (i d) -> p i d", i=NT),
                          a["p_2"][0, 0].rearrange("(i p) d -> p i d", p=P)).then_inc(sig("p_in"), 16)
            take_tile("o0_2", 6, 0)
            take_tile("o1_2", 6, 4)
            squares("x_new", 8, 1)
            root("normm")
            router_exps(2)
            experts(2)
            further(2)
            squares("x_new", 12, 1)
            root("normp")
            take_tile("pg0", 4, 0, func=ACT.Tanh, scale=0.5)
            take_tile("pg1", 4, 4, func=ACT.Tanh, scale=0.5)
            take_tile("pp", 5, 0, groups=4, scale=0.5)
            squares("x_new", 16, 1)
            root("norme")

        @block.vector
        def _(dve):
            steps, n_turn, n_small, n_norm = [0], [0], [0], [0]

            def step(ins):
                steps[0] += 1
                ins.then_inc(sig("dve_steps"), 1)
                dve.wait_ge(sig("dve_steps"), steps[0])

            def small(key):
                assert SAT[key] == n_small[0], key
                n_small[0] += 1
                dve.wait_ge(sig("small_done"), n_small[0])
                return bank[7]

            def small_read(ins):
                ins.then_inc(sig("small_read"), 1)
                dve.wait_ge(sig("small_read"), n_small[0])

            def turns(key, dst):
                n = n_turn[0]
                assert TAT[key] == n, key
                n_turn[0] += 1
                dve.wait_ge(sig("turned"), n + 1)
                dve.tensor_copy(dst, bank[2 + n % 2][:, :]).then_inc(sig("turn_out"), 1)

            def norm(name, gains, dst):
                b = small(name)
                small_read(dve.tensor_scalar(rt[:, :], b[:, 0:T], 1.0 / D, EPS, ALU.mult, ALU.add))
                n_norm[0] += 1
                dve.wait_ge(sig("roots"), n_norm[0])
                step(dve.reciprocal(rt[:, :], rt[:, :]))
                for c in range(DC):
                    dve.scalar_tensor_tensor(dst[:, c, :], xT[:, c, :], gains[:, c:c + 1], rt[:, :],
                                             ALU.mult, ALU.mult).then_inc(sig("scaled"), 1)

            for n, (key, vec) in enumerate((("vecA", vec_a), ("vecB", vec_b))):
                b = small(key)
                small_read(dve.tensor_copy(vec[:, :], b[:, 0:P]))
            b = small("bias")
            small_read(dve.tensor_copy(att_p[0:HEADS, 0:512], b[0:HEADS, :]))
            dve.wait_ge(sig("lam_in"), 64)
            for n in range(2):
                step(dve.tensor_tensor(lam_v[0:1, 2 * n, :], lam_v[0:1, 2 * n, :], lam_v[0:1, 2 * n + 1, :], ALU.mult))
            dve.tensor_reduce(lam_s[0:1, 0:2], lam_v[0:1, 0:4:2, :], AX.X, ALU.add).then_inc(sig("lam_sums"), 1)
            dve.wait_ge(sig("lam_exps"), 1)
            step(dve.tensor_tensor(lam_s[0:1, 5:6], lam_s[0:1, 3:4], lam_s[0:1, 2:3], ALU.subtract))
            dve.tensor_scalar(lam_s[0:1, 4:5], lam_s[0:1, 5:6], -LAM_INIT, None, ALU.add).then_inc(sig("lam_ready"), 1)
            lam_col = ROWS_B["lru_lambda_2"][0]
            lru_lam = vec_b[:, lam_col:lam_col + DC]
            dve.scalar_tensor_tensor(s8[:, 0, :], lru_lam, -1.0, lru_lam, ALU.mult, ALU.max).then_inc(sig("lru_abs"), 1)
            for n, key in ((3, "b_rg_2"), (4, "b_ig_2")):
                c0 = ROWS_B[key][0]
                step(dve.tensor_scalar(s8[:, n, :], vec_b[:, c0:c0 + DC], 0.5, None, ALU.mult))
            c0 = ROWS_B["g_subln_2"][0]
            step(dve.tensor_scalar(sub_gain[:, :], vec_b[:, c0:c0 + 1], 1.0 - LAM_INIT, None, ALU.mult))
            c0 = ROWS_A["b_gate"][0]
            step(dve.tensor_scalar(half_b[:, :], vec_a[:, c0:c0 + 16], 0.5, None, ALU.mult))
            dve.wait_ge(sig("lru_exp"), 1)
            step(dve.tensor_scalar(s8[:, 7, :], s8[:, 1, :], 2.0, None, ALU.add))
            step(dve.reciprocal(s8[:, 7, :], s8[:, 7, :]))
            step(dve.tensor_tensor(s8[:, 1, :], s8[:, 1, :], s8[:, 7, :], ALU.mult))
            step(dve.tensor_tensor(s8[:, 7, :], s8[:, 1, :], s8[:, 1, :], ALU.mult))
            step(dve.tensor_scalar(s8[:, 2, :], s8[:, 7, :], 1.0 / 15, None, ALU.mult))
            for n in (13, 11, 9, 7, 5, 3):
                step(dve.scalar_tensor_tensor(s8[:, 2, :], s8[:, 2, :], 1.0 / n, s8[:, 7, :], ALU.add, ALU.mult))
            step(dve.scalar_tensor_tensor(s8[:, 2, :], s8[:, 2, :], 1.0, s8[:, 1, :], ALU.add, ALU.mult))
            step(dve.tensor_scalar(s8[:, 7, :], lru_lam, -1.0, 0.0, ALU.mult, ALU.max))
            step(dve.scalar_tensor_tensor(s8[:, 2, :], s8[:, 2, :], 2.0, s8[:, 7, :], ALU.mult, ALU.add))
            step(dve.tensor_scalar(s8[:, 5, :], s8[:, 2, :], 0.5 * LRU_C, None, ALU.mult))
            step(dve.tensor_scalar(s8[:, 6, :], s8[:, 2, :], -0.5 * LRU_C, None, ALU.mult))
            dve.wait_ge(sig("consts"), CONSTS)
            step(dve.reciprocal(inv_cnt[:, :], inv_cnt[:, :]))
            b = small("lam")
            small_read(dve.tensor_copy(neg_lam[:, :], b[:, 0:1]))
            for g in range(4):
                turns(("x", g), tile[0][:, g * 512:(g + 1) * 512])

            def modulation(j):
                b = small(f"mod{j}")
                c0 = ROWS_A["b_ada"][0] + 4 * j
                small_read(dve.tensor_tensor(mod[:, 4 * j:4 * j + 4], b[:, 0:4], vec_a[:, c0:c0 + 4], ALU.add))

            for j in range(4):
                modulation(j)
            g0 = ROWS_A["norm1_g"][0]
            step(dve.scalar_tensor_tensor(gain[:, 0, :], mod[:, 8:16], 1.0, vec_a[:, g0:g0 + DC], ALU.add, ALU.mult))
            norm("norm1", gain[:, 0, :], hT)

            def head_1(h):
                dve.wait_ge(sig("scores"), h + 1)
                dve.wait_ge(sig(f"bias_in{h % 2}"), 32 * (h // 2 + 1))
                dve.scalar_tensor_tensor(att_s[:, 0:512], bank[2 + h % 2][:, :], SCALE, bias_sb[h % 2],
                                         ALU.mult, ALU.add).then_inc(sig("scores_read"), 1)
                dve.wait_ge(sig("scores_read"), h + 1)
                dve.tensor_reduce(mx[:, 0:2], att_s[:, 0:512].rearrange("p (i k) -> p i k", k=T), AX.X, ALU.max,
                                  negate=True).then_inc(sig("maxima"), 1)
                dve.wait_ge(sig("exps"), h + 1)
                step(dve.reciprocal(rs[:, 0:2], sm[:, 0:2]))
                for i in range(NT):
                    ins = dve.tensor_scalar(att_p[:, i * T:(i + 1) * T], att_p[:, i * T:(i + 1) * T],
                                            rs[:, i:i + 1], None, ALU.mult)
                ins.then_inc(sig("probs"), 1)

            def add_window(src, dst, g, s):
                dve.tensor_copy(dst[:, g:, 0:s], src[:, g:, 0:s])
                step(dve.tensor_tensor(dst[:, g:, s:T], src[:, g:, s:T], src[:, g:, 0:T - s], ALU.add))

            def pool_means(g, sums):
                w = WINDOWS[g]
                step(dve.tensor_tensor(pool_d[:, g, 0:w], sums[:, g, 0:w], inv_cnt[:, 0:w], ALU.mult))
                step(dve.tensor_scalar(pool_d[:, g, w:T], sums[:, g, w:T], 1.0 / w, None, ALU.mult))
                return dve.tensor_tensor(pool_d[:, g, :], pool_d[:, g, :], u1[:, g, :], ALU.subtract)

            for h in range(HEADS):
                modulation(4 + h)
                head_1(h)
                if 1 <= h <= 4:
                    if h == 1:
                        dve.wait_ge(sig("dense_out"), LAST["u"] + 1)
                    src = u1 if h == 1 else pingpong[h % 2]
                    add_window(src, pingpong[(h + 1) % 2], h - 1, 2 ** (h - 1))
                    ins = pool_means(h - 1, pingpong[(h + 1) % 2])
                    ins.then_inc(sig("pool_parts"), 1)
            g0 = ROWS_A["norm2_g"][0]
            step(dve.scalar_tensor_tensor(gain[:, 1, :], mod[:, 32:40], 1.0, vec_a[:, g0:g0 + DC], ALU.add, ALU.mult))
            for q in range(4):
                cols = slice(q * 512, (q + 1) * 512)
                dve.wait_ge(sig("dense_out"), DAT[("brA", q)] + 1)
                step(dve.scalar_tensor_tensor(tile[4][:, cols], tile[4][:, cols], 1.0, tile[1][:, cols],
                                              ALU.add, ALU.mult))
            for q in range(4):
                cols = slice(q * 512, (q + 1) * 512)
                dve.wait_ge(sig("dense_out"), DAT[("brP", q)] + 1)
                step(dve.scalar_tensor_tensor(tile[5][:, cols], tile[5][:, cols], 1.0, tile[2][:, cols],
                                              ALU.add, ALU.mult))
                dve.tensor_tensor(tile[4][:, cols], tile[4][:, cols], tile[5][:, cols], ALU.add)\
                   .then_inc(sig("mixed"), 1)
            for q in range(4):
                dve.wait_ge(sig("dense_out"), DAT[(f"out{q // 2}", q % 2)] + 1)
                for c in (2 * q, 2 * q + 1):
                    ins = dve.scalar_tensor_tensor(xT[:, c, :], dtile(6)[:, c, :], mod[:, 16 + c:17 + c], xT[:, c, :],
                                                   ALU.mult, ALU.add)
                ins.then_inc(sig("x_new"), 1)

            def first_max(gaps, score, top, onehot):
                w = gaps.shape[2]
                step(dve.scalar_tensor_tensor(score, gaps, 0.0, desc[:, :, 0:w], ALU.is_equal, ALU.mult))
                step(dve.tensor_reduce(top, score, AX.X, ALU.max))
                step(dve.tensor_tensor(onehot, score, spread_out(top, w), ALU.is_equal))

            def spread_out(per_token, w):
                return per_token.unsqueeze(2).to_broadcast([P, NT, w])

            def route(blk):
                for g in range(4):
                    turns((f"h{blk}", g), tile[2][:, g * 512:(g + 1) * 512])
                b = small(f"logit{blk}")
                small_read(dve.tensor_copy(tile[8][:, 264:336], b[:, 0:2 * NLOG]))
                zg4, gap4 = lg[:, :, 0:GROUPS], r8[:, 1, :, 0:GROUPS]
                step(dve.tensor_reduce(r1[:, 0, :], zg4, AX.X, ALU.max))
                dve.tensor_tensor(gap4, zg4, spread_out(r1[:, 0, :], GROUPS), ALU.subtract)\
                   .then_inc(sig("group_gaps"), 1)
                dve.wait_ge(sig("group_gaps"), blk)
                group = r8[:, 3, :, 0:GROUPS]
                first_max(gap4, r8[:, 2, :, 0:GROUPS], r1[:, 11, :], group)
                group_b = group.unsqueeze(3).to_broadcast([P, NT, GROUPS, PER_GROUP])
                step(dve.tensor_tensor(zg, lg[:, :, GROUPS:].rearrange("p i (g e) -> p i g e", g=GROUPS), group_b,
                                       ALU.mult))
                z = r8[:, 4, :, :]
                step(dve.tensor_reduce(z, zg.rearrange("p i g e -> p i e g"), AX.X, ALU.add))
                step(dve.tensor_reduce(r1[:, 3, :], z, AX.X, ALU.max))
                step(dve.tensor_tensor(r8[:, 5, :, :], z, spread_out(r1[:, 3, :], 8), ALU.subtract))
                first, second = r8[:, 6, :, :], r8[:, 9, :, :]
                first_max(r8[:, 5, :, :], r8[:, 2, :, :], r1[:, 11, :], first)
                step(dve.scalar_tensor_tensor(r8[:, 7, :, :], first, FAR, z, ALU.mult, ALU.add))
                step(dve.tensor_reduce(r1[:, 4, :], r8[:, 7, :, :], AX.X, ALU.max))
                dve.tensor_tensor(r1[:, 5, :], r1[:, 4, :], r1[:, 3, :], ALU.subtract).then_inc(sig("pair_gaps"), 1)
                step(dve.tensor_tensor(r8[:, 8, :, :], r8[:, 7, :, :], spread_out(r1[:, 4, :], 8), ALU.subtract))
                first_max(r8[:, 8, :, :], r8[:, 2, :, :], r1[:, 11, :], second)
                dve.wait_ge(sig("group_exps"), blk)
                step(dve.tensor_reduce(r1[:, 1, :], r8[:, 0, :, 0:GROUPS], AX.X, ALU.add))
                step(dve.reciprocal(r1[:, 2, :], r1[:, 1, :]))
                dve.wait_ge(sig("pair_exps"), blk)
                step(dve.tensor_scalar(r1[:, 7, :], r1[:, 6, :], 1.0, None, ALU.add))
                step(dve.reciprocal(r1[:, 8, :], r1[:, 7, :]))
                step(dve.tensor_tensor(r1[:, 9, :], r1[:, 8, :], r1[:, 2, :], ALU.mult))
                step(dve.tensor_tensor(r1[:, 10, :], r1[:, 9, :], r1[:, 6, :], ALU.mult))
                step(dve.tensor_tensor(r8[:, 5, :, :], first, spread_out(r1[:, 9, :], 8), ALU.mult))
                step(dve.tensor_tensor(r8[:, 8, :, :], second, spread_out(r1[:, 10, :], 8), ALU.mult))
                step(dve.tensor_tensor(r8[:, 5, :, :], r8[:, 5, :, :], r8[:, 8, :, :], ALU.add))
                step(dve.tensor_tensor(r8[:, 7, :, :], first, second, ALU.add))

                def by_group(dst, per_group):
                    return dve.tensor_tensor(dst, per_group.unsqueeze(2).to_broadcast([P, NT, GROUPS, PER_GROUP]),
                                             group_b, ALU.mult)

                by_group(sel.rearrange("p i (g e) -> p i g e", g=GROUPS), r8[:, 7, :, :])\
                    .then_inc(sig("sel_ready"), 1)
                step(by_group(comb[:, :, 0:EXPERTS].rearrange("p i (g e) -> p i g e", g=GROUPS), r8[:, 5, :, :]))
                dve.memset(comb[:, :, EXPERTS:], 0.0)
                step(dve.memset(posm[:, :, EXPERTS:], -1.0))
                b = small(f"pos{blk}")
                step(dve.scalar_tensor_tensor(posm[:, :, 0:EXPERTS],
                                              b[:, 0:2 * EXPERTS].rearrange("p (i e) -> p i e", i=NT), 1.0, sel,
                                              ALU.add, ALU.mult))
                step(dve.tensor_scalar(posm[:, :, 0:EXPERTS], posm[:, :, 0:EXPERTS], -1.0, None, ALU.add))
                small_read(dve.tensor_copy(counts, b[:, 2 * EXPERTS:3 * EXPERTS]))

            def list_further(blk):
                for r in range(1, ROUNDS):
                    step(dve.tensor_scalar(ov_more[:, (r - 1) * EXPERTS:r * EXPERTS], counts, float(r * CAP), None,
                                           ALU.is_gt))
                step(dve.tensor_tensor_scan(ov_rank, ones[:, 0:n_code], ov_more, 0.0, ALU.mult, ALU.add))
                dve.tensor_copy(extra[0:1, blk - 1, 0:1], ov_rank[0:1, n_code - 1:n_code])
                step(dve.tensor_tensor(ov_more, ov_more, ov_rank, ALU.mult))
                step(dve.tensor_tensor(ov_hot, ov_more.unsqueeze(1).to_broadcast([P, EXTRA, n_code]),
                                       one_to[:, :].unsqueeze(2).to_broadcast([P, EXTRA, n_code]), ALU.is_equal))
                step(dve.tensor_tensor(ov_hot, ov_hot, code_of[:, :].unsqueeze(1).to_broadcast([P, EXTRA, n_code]),
                                       ALU.mult))
                step(dve.tensor_reduce(ov_code, ov_hot, AX.X, ALU.add))
                step(dve.tensor_scalar(ov_base, ov_code, float(CAP), float(CAP), ALU.is_ge, ALU.mult))
                for r in range(2, ROUNDS):
                    step(dve.tensor_scalar(ov_expert, ov_code, float(r * CAP), float(CAP), ALU.is_ge, ALU.mult))
                    step(dve.tensor_tensor(ov_base, ov_base, ov_expert, ALU.add))
                step(dve.tensor_tensor(ov_expert, ov_code, ov_base, ALU.subtract))
                dve.tensor_copy(extra[0:1, blk - 1, 1:1 + EXTRA], ov_expert[0:1, :]).then_inc(sig(f"extra_{blk}"), 1)
                dve.wait_ge(sig(f"extra_{blk}"), 1)

            def experts(blk):
                def picks(n):
                    for second in range(2):
                        e = n * 2 + second
                        cols = slice(CAP * second, CAP * second + CAP)
                        for i in range(NT):
                            at_e = posm[:, i, bass.ds(e, 1)]
                            dve.tensor_scalar(pick[:, i, cols], iota_cap[:, :], at_e, None, ALU.is_equal)
                            ins = dve.tensor_scalar(pick_w[:, i, cols], iota_cap[:, :], at_e,
                                                    comb[:, i, bass.ds(e, 1)], ALU.is_equal, ALU.mult)
                    ins.then_inc(sig(f"picks_{blk}"), 1)

                picks(0)
                dve.memset(tile[3][:, :], 0.0).then_inc(sig(f"summed_{blk}"), 1)
                list_further(blk)
                with dve.Fori(0, PAIRS // UNROLL) as it:
                    for u in range(UNROLL):
                        at = it * UNROLL + u
                        dve.wait_ge(sig(f"silu_{blk}"), at + 1)
                        dve.wait_ge(sig(f"pe_slots1_{blk}"), at + 1)
                        dve.tensor_tensor(act_u, act_g, bank[1][:, :], ALU.mult).then_inc(sig(f"acts_{blk}"), 1)
                        dve.wait_ge(sig(f"spread_turned_{blk}"), at + 1)
                        dve.tensor_copy(spread, bank[7][:, 0:T]).then_inc(sig(f"spread_{blk}"), 1)
                        dve.wait_ge(sig(f"gathered_{blk}"), at * 2 + 2)
                        picks(at + 1)
                        for q in range(4):
                            cols = slice(q * 512, (q + 1) * 512)
                            dve.wait_ge(sig(f"scattered_{blk}"), at * 4 + (q + 1))
                            dve.tensor_tensor(tile[3][:, cols], tile[3][:, cols], bank[6 + q % 2][:, :], ALU.add)\
                               .then_inc(sig(f"summed_{blk}"), 1)
                dve.wait_ge(sig(f"summed_{blk}"), 4 * PAIRS + 1)

            def further(blk):
                count = dve.value_load(extra[0:1, blk - 1, 0:1], min_val=0, max_val=EXTRA)
                with dve.If(count > 0):
                    dve.wait_ge(sig(f"gathered_{blk}"), 2 * PAIRS + 2)
                    with dve.Fori(0, EXTRA) as j:
                        with dve.If(count > j):
                            further_turn(blk, j)
                        with dve.Else():
                            dve.nop()
                with dve.Else():
                    dve.nop()

            def further_turn(blk, j):
                e = dve.value_load(extra[0:1, blk - 1, bass.ds(j + 1, 1)], min_val=0, max_val=EXPERTS - 1)
                base = ov_base[:, bass.ds(j, 1)]
                for i in range(NT):
                    at_e = posm[:, i, bass.ds(e, 1)]
                    for part in range(2):
                        ins = dve.tensor_scalar(pick[:, i, CAP * part:CAP * part + CAP], iota_cap[:, :], base, at_e,
                                                ALU.add, ALU.is_equal)
                ins.then_inc(sig(f"ov_hot_{blk}"), 1)
                dve.wait_ge(sig(f"ov_hot_{blk}"), j + 1)
                for i in range(NT):
                    ins = dve.tensor_scalar(pick_w[:, i, :], pick[:, i, :], comb[:, i, bass.ds(e, 1)], None, ALU.mult)
                ins.then_inc(sig(f"ov_picks_{blk}"), 1)
                dve.wait_ge(sig(f"ov_spread_turned_{blk}"), j + 1)
                dve.tensor_copy(spread, bank[7][:, 0:T]).then_inc(sig(f"ov_spread_{blk}"), 1)
                dve.wait_ge(sig(f"ov_silu_{blk}"), j + 1)
                dve.tensor_tensor(act_u[:, 0:256], act_g[:, 0:256], bank[1][:, 0:256], ALU.mult)\
                   .then_inc(sig(f"ov_acts_{blk}"), 1)
                for q in range(4):
                    cols = slice(q * 512, (q + 1) * 512)
                    dve.wait_ge(sig(f"ov_scattered_{blk}"), j * 4 + (q + 1))
                    dve.tensor_tensor(tile[3][:, cols], tile[3][:, cols], bank[6 + q % 2][:, :], ALU.add)\
                       .then_inc(sig(f"ov_summed_{blk}"), 1)
                dve.wait_ge(sig(f"ov_summed_{blk}"), j * 4 + 4)
                dve.memset(pick_w[:, 0, 0:1], 0.0)

            norm("norm2", gain[:, 1, :], hT)
            route(1)
            experts(1)
            further(1)
            for q in range(4):
                for c in (2 * q, 2 * q + 1):
                    ins = dve.scalar_tensor_tensor(xT[:, c, :], yacc[:, c, :], mod[:, 40 + c:41 + c], xT[:, c, :],
                                                   ALU.mult, ALU.add)
                ins.then_inc(sig("x_new"), 1)
            dve.wait_ge(sig("x_new"), 8)
            g0 = ROWS_A["norm_f_g"][0]
            norm("normf", vec_a[:, g0:g0 + DC], xT)
            dve.wait_ge(sig("scaled"), 3 * DC)
            g0 = ROWS_B["g_mix_2"][0]
            norm("normx", vec_b[:, g0:g0 + DC], hT)

            def head_2(h):
                n = HEADS + h
                dve.wait_ge(sig("scores"), n + 1)
                for c in range(2):
                    ins = dve.scalar_tensor_tensor(att_s[:, c * 512:(c + 1) * 512], bank[2 + c][:, :], SCALE,
                                                   mask[:, :, :].rearrange("p i k -> p (i k)"), ALU.mult, ALU.add)
                ins.then_inc(sig("scores_read"), 1)
                dve.wait_ge(sig("scores_read"), n + 1)
                dve.tensor_reduce(mx[:, 0:4], att_s[:, :].rearrange("p (i k) -> p i k", k=T), AX.X, ALU.max,
                                  negate=True).then_inc(sig("maxima"), 1)
                dve.wait_ge(sig("exps"), n + 1)
                step(dve.reciprocal(rs[:, :], sm[:, :]))
                step(dve.tensor_scalar(rs[:, 2:4], rs[:, 2:4], neg_lam[:, 0:1], None, ALU.mult))
                for i in range(NT):
                    b = att_p[:, (2 + i) * T:(3 + i) * T]
                    step(dve.tensor_scalar(b, b, rs[:, 2 + i:3 + i], None, ALU.mult))
                for i in range(NT):
                    p0, p1 = att_p[:, i * T:(i + 1) * T], att_p[:, (2 + i) * T:(3 + i) * T]
                    ins = dve.scalar_tensor_tensor(p0, p0, rs[:, i:i + 1], p1, ALU.mult, ALU.add)
                ins.then_inc(sig("probs"), 1)

            def conv(c):
                dve.wait_ge(sig("dense_out"), DAT[(f"xr{c // 4}_2", (c % 4) // 2)] + 1)
                w0, b0 = ROWS_B["w_conv_2"][0], ROWS_B["b_conv_2"][0]
                step(dve.tensor_scalar(xc[:, c, :], xr[:, c, :], vec_b[:, w0 + 3 * DC + c:w0 + 3 * DC + c + 1],
                                       vec_b[:, b0 + c:b0 + c + 1], ALU.mult, ALU.add))
                for s in range(1, 4):
                    tap = w0 + (3 - s) * DC + c
                    ins = dve.scalar_tensor_tensor(xc[:, c, s:T], xr[:, c, 0:T - s], vec_b[:, tap:tap + 1],
                                                   xc[:, c, s:T], ALU.mult, ALU.add)
                    if s < 3:
                        step(ins)
                ins.then_inc(sig("conv"), 1)

            for h in range(HEADS):
                head_2(h)
                conv(h)
            for g in range(4):
                b = small(f"sub{g}")
                small_read(dve.tensor_scalar(sub_r[g % 2], b[:, :], 1.0 / P, EPS_SUB, ALU.mult, ALU.add))
                dve.wait_ge(sig("sub_roots"), g + 1)
                step(dve.reciprocal(sub_r[g % 2], sub_r[g % 2]))
                cols = slice(g * 512, (g + 1) * 512)
                dve.scalar_tensor_tensor(tile[2][:, cols], tile[2][:, cols], sub_gain[:, 0:1], sub_r[g % 2],
                                         ALU.mult, ALU.mult).then_inc(sig("o_normed"), 1)

            def gate_branch(n):
                t, q = 7 + n // 4, n % 4
                cols = slice(q * 512, (q + 1) * 512)
                dve.wait_ge(sig("dense_out"), DAT[(STREAM2[14 + n // 2], n % 2)] + 1)
                dve.scalar_tensor_tensor(tile[t][:, cols], tile[t][:, cols], 1.0, ev[:, n % 2, :],
                                         ALU.add, ALU.mult).then_inc(sig("branch_read"), 1)

            dve.wait_ge(sig("lru_t"), DC)
            for n in range(2):
                cols = slice(n * 1024, (n + 1) * 1024)
                one_t = (att_s, att_p)[n][:, :]
                step(dve.tensor_scalar(one_t, tile[5][:, cols], 1.0, None, ALU.add))
                step(dve.reciprocal(one_t, one_t))
                dve.scalar_tensor_tensor(tile[5][:, cols], tile[5][:, cols], 2.0, one_t, ALU.mult, ALU.mult)\
                   .then_inc(sig("lru_frac"), 1)
            gate_branch(0)
            step(dve.memset(lru_a[:, :, 0:1], 0.0))
            for n in range(2):
                cols = slice(n * 1024, (n + 1) * 1024)
                step(dve.scalar_tensor_tensor(tile[4][:, cols], tile[4][:, cols], 1.0, tile[3][:, cols],
                                              ALU.add, ALU.mult))
                dve.wait_ge(sig("lru_mult"), n + 1)
                step(dve.scalar_tensor_tensor(tile[4][:, cols], tile[4][:, cols], 0.5, tile[5][:, cols],
                                              ALU.mult, ALU.mult))
            gate_branch(1)
            step(dve.tensor_tensor_scan(tile[5][:, :], tile[1][:, :], tile[4][:, :], 0.0, ALU.mult, ALU.add))
            dve.wait_ge(sig("gelu"), 1)
            dve.tensor_tensor(tile[1][:, :], tile[5][:, :], tile[6][:, :], ALU.mult).then_inc(sig("lru_y"), 1)
            for n in range(2, 8):
                gate_branch(n)
                if n >= 4:
                    cols = slice((n - 4) * 512, (n - 3) * 512)
                    dve.wait_ge(sig("branch_read"), n + 1)
                    dve.tensor_tensor(tile[7][:, cols], tile[7][:, cols], tile[8][:, cols], ALU.add)\
                       .then_inc(sig("mixed"), 1)
            for q in range(4):
                cols = slice(q * 512, (q + 1) * 512)
                dve.wait_ge(sig("dense_out"), DAT[(f"o{q // 2}_2", q % 2)] + 1)
                dve.tensor_tensor(tile[0][:, cols], tile[0][:, cols], tile[6][:, cols], ALU.add)\
                   .then_inc(sig("x_new"), 1)
            dve.wait_ge(sig("x_new"), 12)
            g0 = ROWS_B["g_moe_2"][0]
            norm("normm", vec_b[:, g0:g0 + DC], hT)
            route(2)
            experts(2)
            further(2)
            for q in range(4):
                cols = slice(q * 512, (q + 1) * 512)
                dve.tensor_tensor(tile[0][:, cols], tile[0][:, cols], tile[3][:, cols], ALU.add)\
                   .then_inc(sig("x_new"), 1)
            dve.wait_ge(sig("x_new"), 16)
            g0 = ROWS_B["g_ple_2"][0]
            norm("normp", vec_b[:, g0:g0 + DC], hT)
            turns(("p", 0), att_p[:, 0:512])
            for q in range(4):
                cols = slice(q * 512, (q + 1) * 512)
                dve.wait_ge(sig("dense_out"), DAT[("pp", q)] + 1)
                step(dve.scalar_tensor_tensor(tile[4][:, cols], tile[4][:, cols], 1.0, tile[5][:, cols],
                                              ALU.add, ALU.mult))
                dve.tensor_tensor(tile[0][:, cols], tile[0][:, cols], tile[4][:, cols], ALU.add)\
                   .then_inc(sig("x_new"), 1)
            dve.wait_ge(sig("x_new"), 20)
            g0 = ROWS_B["g_final_2"][0]
            norm("norme", vec_b[:, g0:g0 + DC], hT)
            for g in range(4):
                turns(("y", g), tile[2][:, g * 512:(g + 1) * 512])


def bucket_rows():
    import math

    import numpy as np

    rows = np.zeros((BUCKETS + 1, 512), np.float32)
    exact = BUCKETS // 2
    for col in range(511):
        n = T - 1 - col
        if n < 0:
            rows[0, col], rows[BUCKETS, col] = 1.0, FAR
            continue
        far = exact + int(math.log(max(n, 1) / exact) / math.log(128 / exact) * (BUCKETS - exact) + 1e-9)
        rows[n if n < exact else min(far, BUCKETS - 1), col] = 1.0
    return rows


INPUTS = [
    "x", "c", "w_ada", "b_ada", "norm1_g", "w_in", "b_gate", "rel_bias", "pool_w", "pool_scale", "w_branch_attn",
    "w_branch_pool", "w_out", "norm2_g", "w_router_group", "b_router_group", "w_router_expert", "b_router_expert",
    "w_expert_gate", "w_expert_up", "w_expert_down", "norm_f_g", "p_2", "g_mix_2", "w_in_2", "lam_q1_2", "lam_k1_2",
    "lam_q2_2", "lam_k2_2", "g_subln_2", "w_conv_2", "b_conv_2", "w_rg_2", "b_rg_2", "w_ig_2", "b_ig_2",
    "lru_lambda_2", "w_attn_br_2", "w_lru_br_2", "w_out_2", "g_moe_2", "w_rt_group_2", "b_rt_group_2",
    "w_rt_expert_2", "b_rt_expert_2", "w_e_gate_2", "w_e_up_2", "w_e_down_2", "g_ple_2", "w_ple_gate_2",
    "w_ple_proj_2", "g_final_2",
]


def kernel(**inputs):
    import concourse.bacc as bacc
    import numpy as np
    from concourse.bass_utils import run_bass_kernel_spmd

    nc = bacc.Bacc("TRN2", target_bir_lowering=False, num_devices=1, dynamic_dma_scratch_size=1024)
    arrays = {f"in_{name}": np.ascontiguousarray(inputs[name]) for name in INPUTS}
    arrays["in_bucket_rows"] = bucket_rows()
    aps = {name[3:]: nc.dram_tensor(name, v.shape, mybir.dt.from_np(v.dtype), kind="ExternalInput").ap()
           for name, v in arrays.items()}
    out = nc.dram_tensor("out", (1, T, D), F32, kind="ExternalOutput").ap()
    build(nc, aps, out)
    result = run_bass_kernel_spmd(nc, [arrays], core_ids=[0])
    return result.results[0]["out"]
```
